# Optimizing a Trainium2 kernel written in Bass

```python
import math
import jax
import jax.numpy as jnp
from jax import lax
import numpy as np

D_MODEL = 1024
BATCH = 1
SEQ = 128
DEPTH = 1
DEC_BATCH = 1
DEC_SEQ = 256
PAST_LEN = 128

GRID_W = 64
EPS = 1e-6
DA_HEADS = 4
DA_DH = 64
DA_WIDTH = DA_HEADS * 2 * DA_DH
ROPE_BASE = 10000.0
ROPE_F = DA_DH // 4
Q_BLOCK = 128
DN_HEADS = 4
DN_DK = 128
DN_DV = 128
DN_WIDTH = DN_HEADS * DN_DV
DN_CONV = 5
DN_CONV_CH = 2 * DN_HEADS * DN_DK + DN_WIDTH
DN_CHUNK = 64
MIX_WIDTH = DA_WIDTH + DN_WIDTH
IN_SIZES = (DA_WIDTH, DA_WIDTH, DA_WIDTH, DN_HEADS * DN_DK, DN_HEADS * DN_DK, DN_WIDTH, DN_WIDTH, 2 * DN_HEADS, 2 * DN_HEADS)
IN_WIDTH = sum(IN_SIZES)
IN_OFFSETS = tuple(int(o) for o in np.cumsum(IN_SIZES)[:-1])
PEER_HEADS = 8
PEER_DK = 256
N_KEYS = 128
N_EXPERTS = N_KEYS * N_KEYS
PEER_TOPK = 16

kernel_name = 'hybrid_diffattn_gdn_peer_diffusion_step'

def rmsnorm(x, g):
    xf = x.astype(jnp.float32)
    y = xf * lax.rsqrt(jnp.mean(xf * xf, axis=-1, keepdims=True) + EPS)
    return (y * g.astype(jnp.float32)).astype(x.dtype)

def l2norm(x):
    xf = x.astype(jnp.float32)
    return xf * lax.rsqrt(jnp.sum(xf * xf, axis=-1, keepdims=True) + EPS)

def axial_rope_tables(n, dtype):
    rows = n // GRID_W
    r, col = jnp.meshgrid(jnp.arange(rows), jnp.arange(GRID_W), indexing='ij')
    pos = jnp.stack([r.reshape(-1), col.reshape(-1)], axis=-1).astype(jnp.float32)
    inv = jnp.power(ROPE_BASE, -jnp.arange(0, 2 * ROPE_F, 2, dtype=jnp.float32) / (2 * ROPE_F))
    ang = pos[:, :, None] * inv
    return jnp.cos(ang).astype(dtype), jnp.sin(ang).astype(dtype)

def apply_axial_rope(x, cos, sin):
    B, n, H, _ = x.shape
    x6 = x.reshape(B, n, H, 2, 2, ROPE_F)
    x1, x2 = x6[..., 0, :], x6[..., 1, :]
    c = cos[None, :, None]
    s = sin[None, :, None]
    out = jnp.stack([x1 * c - x2 * s, x2 * c + x1 * s], axis=-2)
    return out.reshape(x.shape)

def diff_attention(q, k, v, lam):
    B, Sq = q.shape[0], q.shape[1]
    nb = Sq // Q_BLOCK
    qb = jnp.swapaxes(q.reshape(B, nb, Q_BLOCK, 2 * DA_HEADS, DA_DH), 0, 1)
    scale = DA_DH ** -0.5

    def one_block(qblk):
        s = jnp.einsum('bqhd,bkhd->bhqk', qblk, k).astype(jnp.float32) * scale
        p = jax.nn.softmax(s, axis=-1).reshape(B, DA_HEADS, 2, Q_BLOCK, s.shape[-1])
        a = p[:, :, 0] - lam * p[:, :, 1]
        return jnp.einsum('bhqk,bkhe->bqhe', a.astype(v.dtype), v)

    out = lax.map(one_block, qb)
    return jnp.swapaxes(out, 0, 1).reshape(B, Sq, DA_HEADS, 2 * DA_DH)

def short_conv(x, w):
    C = x.shape[-1]
    y = lax.conv_general_dilated(x, w[:, None, :].astype(x.dtype), window_strides=(1,),
                                 padding=[(DN_CONV // 2, DN_CONV // 2)],
                                 dimension_numbers=('NWC', 'WIO', 'NWC'), feature_group_count=C)
    return jax.nn.silu(y)

def gated_delta_chunked(q, k, v, beta, g, s0):
    B, S, H, _ = q.shape
    DV = v.shape[-1]
    C = DN_CHUNK
    n = S // C
    f32 = jnp.float32

    def chunks(t):
        t = t.astype(f32).reshape((B, n, C, H) + t.shape[3:])
        return jnp.swapaxes(jnp.swapaxes(t, 0, 1), 2, 3)

    qc, kc, vc, bc = chunks(q), chunks(k), chunks(v), chunks(beta)
    gcum = jnp.cumsum(chunks(g), axis=-1)
    tril = jnp.tril(jnp.ones((C, C), dtype=bool))
    strict = jnp.tril(jnp.ones((C, C), dtype=bool), k=-1)
    decay = jnp.exp(jnp.where(tril, gcum[..., :, None] - gcum[..., None, :], -jnp.inf))
    kb = kc * bc[..., None]
    lmat = jnp.where(strict, jnp.einsum('nbhid,nbhjd->nbhij', kb, kc) * decay, 0.0)
    eye = jnp.broadcast_to(jnp.eye(C, dtype=f32), lmat.shape)
    tmat = lax.linalg.triangular_solve(eye + lmat, eye, left_side=True, lower=True, unit_diagonal=True)
    u = jnp.einsum('nbhij,nbhjd->nbhid', tmat, vc * bc[..., None])
    w = jnp.einsum('nbhij,nbhjd->nbhid', tmat, kb * jnp.exp(gcum)[..., None])
    a_intra = jnp.where(tril, jnp.einsum('nbhid,nbhjd->nbhij', qc, kc) * decay, 0.0)

    def step(state, xs):
        q_i, k_i, u_i, w_i, a_i, g_i = xs
        v_new = u_i - jnp.einsum('bhck,bhkv->bhcv', w_i, state)
        o_i = (jnp.einsum('bhck,bhkv->bhcv', q_i * jnp.exp(g_i)[..., None], state)
               + jnp.einsum('bhij,bhjv->bhiv', a_i, v_new))
        g_last = g_i[..., -1:]
        state = (state * jnp.exp(g_last)[..., None]
                 + jnp.einsum('bhck,bhcv->bhkv', k_i * jnp.exp(g_last - g_i)[..., None], v_new))
        return state, o_i

    s_fin, o = lax.scan(step, s0.astype(f32), (qc, kc, u, w, a_intra, gcum))
    o = jnp.swapaxes(jnp.swapaxes(o, 0, 1), 2, 3).reshape(B, S, H, DV)
    return o.astype(v.dtype), s_fin.astype(s0.dtype)

def reverse_time(t):
    return jnp.flip(t, axis=1)

def deltanet_mixer(dq, dk, dv, dz, db, da, conv_w, a_log, dt_bias, dn_norm, s0_f, s0_b):
    B, S, _ = dq.shape
    qkv = short_conv(jnp.concatenate([dq, dk, dv], axis=-1), conv_w)
    q, k, v = jnp.split(qkv, [DN_HEADS * DN_DK, 2 * DN_HEADS * DN_DK], axis=-1)
    q = l2norm(q.reshape(B, S, DN_HEADS, DN_DK)) * (DN_DK ** -0.5)
    k = l2norm(k.reshape(B, S, DN_HEADS, DN_DK))
    v = v.reshape(B, S, DN_HEADS, DN_DV)
    beta = jax.nn.sigmoid(db.astype(jnp.float32)).reshape(B, S, 2, DN_HEADS)
    g = -jnp.exp(a_log.astype(jnp.float32)) * jax.nn.softplus(
        da.astype(jnp.float32).reshape(B, S, 2, DN_HEADS) + dt_bias.astype(jnp.float32))
    o_f, s_f = gated_delta_chunked(q, k, v, beta[:, :, 0], g[:, :, 0], s0_f)
    o_b, s_b = gated_delta_chunked(reverse_time(q), reverse_time(k), reverse_time(v),
                                   reverse_time(beta[:, :, 1]), reverse_time(g[:, :, 1]), s0_b)
    o = o_f + reverse_time(o_b)
    o = rmsnorm(o, dn_norm) * jax.nn.silu(dz.reshape(B, S, DN_HEADS, DN_DV))
    return o.reshape(B, S, DN_WIDTH), s_f, s_b

def peer(h, w_pq, sub_keys, expert_u, expert_v):
    B, S, D = h.shape
    T = B * S
    hf = h.reshape(T, D)
    q = (hf @ w_pq).reshape(T, PEER_HEADS, 2, PEER_DK // 2)
    s = jnp.einsum('thpd,hpnd->thpn', q, sub_keys).astype(jnp.float32)
    sv, si = lax.top_k(s, PEER_TOPK)
    cand = (sv[:, :, 0, :, None] + sv[:, :, 1, None, :]).reshape(T, PEER_HEADS, PEER_TOPK * PEER_TOPK)
    cidx = (si[:, :, 0, :, None] * N_KEYS + si[:, :, 1, None, :]).reshape(T, PEER_HEADS, PEER_TOPK * PEER_TOPK)
    top_s, pos = lax.top_k(cand, PEER_TOPK)
    eidx = jnp.take_along_axis(cidx, pos, axis=-1).reshape(T, PEER_HEADS * PEER_TOPK)
    gates = jax.nn.softmax(top_s, axis=-1).reshape(T, PEER_HEADS * PEER_TOPK)
    act = jnp.einsum('td,nd->tn', hf, expert_u)
    a_sel = jnp.take_along_axis(act, eidx, axis=1).astype(jnp.float32)
    coef = (gates * jax.nn.gelu(a_sel, approximate=False)).astype(h.dtype)
    dense = jnp.zeros((T, N_EXPERTS), h.dtype).at[jnp.arange(T)[:, None], eidx].add(coef)
    return (dense @ expert_v).reshape(B, S, D)

def layer(x, cvec, lw, lam_init, rope, ctx):
    (w_mod, b_mod, norm_attn, norm_ffn, w_in, conv_w, a_log, dt_bias, dn_norm,
     lambda_q1, lambda_k1, lambda_q2, lambda_k2, subln, w_out, w_pq, sub_keys,
     expert_u, expert_v) = lw
    B, S, _ = x.shape
    f32 = jnp.float32
    mod = jax.nn.silu(cvec) @ w_mod + b_mod
    sh_a, sc_a, g_a, sh_f, sc_f, g_f = [m[:, None, :] for m in jnp.split(mod, 6, axis=-1)]
    h = rmsnorm(x, norm_attn) * (1.0 + sc_a) + sh_a
    da_q, da_k, da_v, dn_q, dn_k, dn_v, dn_z, dn_b, dn_a = jnp.split(h @ w_in, IN_OFFSETS, axis=-1)
    q = da_q.reshape(B, S, 2 * DA_HEADS, DA_DH)
    k = da_k.reshape(B, S, 2 * DA_HEADS, DA_DH)
    v = da_v.reshape(B, S, DA_HEADS, 2 * DA_DH)
    lam = (jnp.exp(jnp.sum(lambda_q1.astype(f32) * lambda_k1.astype(f32)))
           - jnp.exp(jnp.sum(lambda_q2.astype(f32) * lambda_k2.astype(f32))) + lam_init)
    if ctx is None:
        keys, vals = k, v
        s0_f = jnp.zeros((B, DN_HEADS, DN_DK, DN_DV), x.dtype)
        s0_b = jnp.zeros((B, DN_HEADS, DN_DK, DN_DV), x.dtype)
    else:
        ctx_k, ctx_v, s0_f, s0_b = ctx
        cos, sin = rope
        q = apply_axial_rope(q, cos, sin)
        keys = jnp.concatenate([ctx_k, apply_axial_rope(k, cos, sin)], axis=1)
        vals = jnp.concatenate([ctx_v, v], axis=1)
    o_da = diff_attention(q, keys, vals, lam)
    o_da = (rmsnorm(o_da, subln) * (1.0 - lam_init)).reshape(B, S, DA_WIDTH)
    o_dn, s_f, s_b = deltanet_mixer(dn_q, dn_k, dn_v, dn_z, dn_b, dn_a, conv_w, a_log, dt_bias,
                                    dn_norm, s0_f, s0_b)
    x = x + g_a * (jnp.concatenate([o_da, o_dn], axis=-1) @ w_out)
    h = rmsnorm(x, norm_ffn) * (1.0 + sc_f) + sh_f
    x = x + g_f * peer(h, w_pq, sub_keys, expert_u, expert_v)
    return x, k, v, s_f, s_b

def _normal(k, shape, scale):
    return jax.random.normal(k, shape, jnp.float32) * scale

def setup_inputs(seed: int = 0) -> dict:
    key = jax.random.key(seed)
    ks = jax.random.split(key, 32)
    f32 = jnp.float32
    dt = jnp.exp(jax.random.uniform(ks[14], (DEPTH, 2, DN_HEADS), f32, math.log(1e-3), math.log(1e-1)))
    return {
        'x_prompt': _normal(ks[0], (BATCH, SEQ, D_MODEL), 1.0),
        'x_sample': _normal(ks[1], (DEC_BATCH, DEC_SEQ, D_MODEL), 1.0),
        'cache_k': _normal(ks[2], (DEC_BATCH, DEPTH, PAST_LEN, 2 * DA_HEADS, DA_DH), 1.0),
        'cache_v': _normal(ks[3], (DEC_BATCH, DEPTH, PAST_LEN, DA_HEADS, 2 * DA_DH), 1.0),
        'state_fwd': _normal(ks[4], (DEC_BATCH, DEPTH, DN_HEADS, DN_DK, DN_DV), 0.1),
        'state_bwd': _normal(ks[5], (DEC_BATCH, DEPTH, DN_HEADS, DN_DK, DN_DV), 0.1),
        'c': _normal(ks[6], (DEC_BATCH, D_MODEL), 1.0),
        'c_ctx': _normal(ks[7], (D_MODEL,), 1.0),
        'w_mod': _normal(ks[8], (DEPTH, D_MODEL, 6 * D_MODEL), 0.5 * D_MODEL ** -0.5),
        'b_mod': _normal(ks[9], (DEPTH, 6 * D_MODEL), 0.02),
        'norm_attn': 1.0 + _normal(ks[10], (DEPTH, D_MODEL), 0.02),
        'norm_ffn': 1.0 + _normal(ks[11], (DEPTH, D_MODEL), 0.02),
        'w_in': _normal(ks[12], (DEPTH, D_MODEL, IN_WIDTH), D_MODEL ** -0.5),
        'conv_w': _normal(ks[13], (DEPTH, DN_CONV, DN_CONV_CH), DN_CONV ** -0.5),
        'a_log': jnp.log(jax.random.uniform(ks[15], (DEPTH, 2, DN_HEADS), f32, 1.0, 16.0)),
        'dt_bias': dt + jnp.log(-jnp.expm1(-dt)),
        'dn_norm': 1.0 + _normal(ks[16], (DEPTH, DN_DV), 0.02),
        'lambda_q1': _normal(ks[17], (DEPTH, DA_DH), 0.1),
        'lambda_k1': _normal(ks[18], (DEPTH, DA_DH), 0.1),
        'lambda_q2': _normal(ks[19], (DEPTH, DA_DH), 0.1),
        'lambda_k2': _normal(ks[20], (DEPTH, DA_DH), 0.1),
        'subln': 1.0 + _normal(ks[21], (DEPTH, 2 * DA_DH), 0.02),
        'w_out': _normal(ks[22], (DEPTH, MIX_WIDTH, D_MODEL), MIX_WIDTH ** -0.5),
        'w_pq': _normal(ks[23], (DEPTH, D_MODEL, PEER_HEADS * PEER_DK), D_MODEL ** -0.5),
        'sub_keys': _normal(ks[24], (DEPTH, PEER_HEADS, 2, N_KEYS, PEER_DK // 2), (PEER_DK // 2) ** -0.5),
        'expert_u': _normal(ks[25], (DEPTH, N_EXPERTS, D_MODEL), D_MODEL ** -0.5),
        'expert_v': _normal(ks[26], (DEPTH, N_EXPERTS, D_MODEL), 0.5),
        'norm_out': 1.0 + _normal(ks[27], (D_MODEL,), 0.02),
    }

def reference(x_prompt, x_sample, cache_k, cache_v, state_fwd, state_bwd, c, c_ctx,
              w_mod, b_mod, norm_attn, norm_ffn, w_in, conv_w, a_log, dt_bias, dn_norm,
              lambda_q1, lambda_k1, lambda_q2, lambda_k2, subln, w_out, w_pq, sub_keys,
              expert_u, expert_v, norm_out):
    rope = axial_rope_tables(x_sample.shape[1], x_sample.dtype)
    xp = x_prompt
    xs = x_sample
    ks_list, vs_list, sf_list, sb_list = [], [], [], []
    for l in range(DEPTH):
        lw = (w_mod[l], b_mod[l], norm_attn[l], norm_ffn[l], w_in[l], conv_w[l], a_log[l],
              dt_bias[l], dn_norm[l], lambda_q1[l], lambda_k1[l], lambda_q2[l], lambda_k2[l],
              subln[l], w_out[l], w_pq[l], sub_keys[l], expert_u[l], expert_v[l])
        lam_init = 0.8 - 0.6 * math.exp(-0.3 * l)
        xp, k_ctx, v_ctx, s_f, s_b = layer(xp, c_ctx[None, :], lw, lam_init, None, None)
        ks_list.append(k_ctx)
        vs_list.append(v_ctx)
        sf_list.append(s_f)
        sb_list.append(s_b)
        xs, _, _, _, _ = layer(xs, c, lw, lam_init, rope,
                               (cache_k[:, l], cache_v[:, l], state_fwd[:, l], state_bwd[:, l]))
    y_prompt = rmsnorm(xp, norm_out)
    y_sample = rmsnorm(xs, norm_out)
    new_cache_k = jnp.stack(ks_list, axis=1)
    new_cache_v = jnp.stack(vs_list, axis=1)
    new_state_fwd = jnp.stack(sf_list, axis=1)
    new_state_bwd = jnp.stack(sb_list, axis=1)
    return (y_prompt, y_sample, new_cache_k, new_cache_v, new_state_fwd, new_state_bwd)


_drawn_inputs = setup_inputs


def setup_inputs(seed=0):
    import zlib

    import numpy as np

    out = dict(_drawn_inputs(seed))
    spreads = {}
    factors = {'state_fwd': 4.344,
     'state_bwd': 5.148,
     'norm_ffn': 18.591,
     'dn_norm': 24.405,
     'lambda_q1': 6.33,
     'lambda_k1': 180.312,
     'lambda_q2': 8.0,
     'lambda_k2': 8.0,
     'subln': 48.216,
     'norm_out': 27.679}
    for name, (base, spread) in spreads.items():
        noise = np.random.default_rng([zlib.crc32(name.encode()), seed]).standard_normal(out[name].shape)
        drawn = base * np.exp(spread * noise) if base else spread * noise
        out[name] = jnp.asarray(drawn.astype(out[name].dtype))
    for name, factor in factors.items():
        out[name] = (out[name] * factor).astype(out[name].dtype)
    return out
```

```python
import numpy as np
import concourse.bass as bass
from concourse import mybir
from contextlib import ExitStack

P = 128
D = 1024
KD = D // P
NT = 3
T = NT * P
DA_H, DA_DH = 4, 64
DN_H = 4
PEER_H, NKEY, TOPK = 8, 128, 16
SLOTS = PEER_H * TOPK
CH = 512
EPS = 1e-6
LAM_INIT = 0.2
GRID_W = 64
TAPS = 5
LEVELS = 7
BIG = 1e30
BF16_ONE = 0x3F80
NEG = -3.0e38

C_ID, C_UP, C_LO, C_NBF, C_NBB = 0, 128, 256, 384, 512
C_COS = 640
C_SIN = C_COS + 64
C_IOTA = C_SIN + 64
C_END = C_IOTA + 16
Q_C, Q_BMOD, Q_NA, Q_NF, Q_CONV = 0, 16, 64, 72, 80
Q_DNN, Q_SUB, Q_ALOG, Q_DT, Q_LAM = 140, 268, 396, 404, 412
Q_END = 668

CHUNKS = ([("mod", m, 0) for m in range(4)] + [("dn", i, 0) for i in range(3)] + [("z", 0, 0)]
          + [("da", c, 0) for c in (2, 0, 1)] + [("mod", m, 0) for m in range(4, 12)]
          + [c for ps in range(2) for c in [("out", 0, ps), ("out", 1, ps)] + [("pq", i, ps) for i in range(4)]])
CHUNK_NO = {c: n for n, c in enumerate(CHUNKS)}
STORED = [c for c in CHUNKS if c[2] == 0]
WSLOTS = 2

PAIRS = [[(0, 0), (0, 1)], [(1, 0), (2, 1)], [(2, 0), (1, 1)]]

GU = 1
GR = 6
NG = SLOTS // GU
ROUNDS = (NG - 2) // GR
REST = range(1 + ROUNDS * GR, NG)
RING0, RINGN = 2, 6


class Counts:

    def __init__(self):
        self.at = {}
        self.jobs = {}
        self.release = {}


class Signal:

    def __init__(self, sem, name, counts):
        self.sem, self.name, self.counts, self.n = sem, name, counts, 0

    def next(self, *key):
        self.n += 1
        self.counts.at[(self.name,) + key] = self.n
        return self.sem, 1

    def at(self, *key):
        return self.sem, self.counts.at.get((self.name,) + key, 1)


def weave(steps, between):
    out, n = [], 0
    for i, s in enumerate(steps):
        out.append(s)
        while n < len(between) and n * len(steps) < (i + 1) * len(between):
            out.append(between[n])
            n += 1
    return out + between[n:]


def deltanet(p):
    out = [("dn_scale", p), ("dn_decay", p), ("dn_scores", p)]
    for lv in range(LEVELS):
        out += [("dn_p", p, lv), ("dn_t", p, lv)]
    return out + [("dn_w", p), ("dn_v", p), ("dn_o", p), ("dn_s", p)]


def attention(t):
    out = []
    for k in range(DA_H + 3):
        for lag, names in ((2, ("a_copy",)), (3, ("v_copy",)), (0, ("score", "expo")), (2, ("value",)),
                           (1, ("diff", "a_turn"))):
            if 0 <= k - lag < DA_H:
                out += [(n, t, k - lag) for n in names]
        out.append(("seam",))
    return out


def output(t):
    return [("head_norm", t, 0), ("seam",), ("head_norm", t, 1), ("o_turn", t), ("seam",), ("o_copy", t),
            ("w_out", t, 0), ("seam",), ("w_out", t, 1), ("resid", t, 0), ("seam",), ("resid", t, 1), ("norm", 1, t),
            ("seam",), ("x_turn", 1, t), ("seam",), ("x_copy", 1, t), ("h_turn", t), ("seam",), ("h_copy", t),
            ("seam",)]


def retrieval(tiles):
    units = [(i, t) for i in range(4) for t in tiles]
    out = []
    for k in range(len(units) + 3):
        for lag, names in ((0, ("query",)), (1, ("q_copy", "key_score")), (2, ("s_copy",)), (3, ("top_key",))):
            if 0 <= k - lag < len(units):
                out += [(n,) + units[k - lag] for n in names]
        out.append(("seam",))
    for t in tiles:
        for hh in range(2):
            out += [("top_pair", t, hh), ("seam",), ("experts", t, hh), ("seam",)]
        out += [("slot_gates", t), ("seam",)]
    return out


def parts(steps):
    out, part = [], []
    for s in steps + [("seam",)]:
        if s[0] == "seam":
            out += [part] * bool(part)
            part = []
        else:
            part.append(s)
    return out


def alone(steps):
    return [[s] for s in steps]


def flat(lists):
    return [s for part in lists for s in part]


def schedule():
    out = [("norm", 0, 0)] + [("mod", m) for m in range(4)] + [("scales", 0)]
    for t in range(NT):
        out += ([("norm", 0, t)] if t else []) + [("x_turn", 0, t), ("x_copy", 0, t)]
    for b in range(14):
        out += [("channels", b)] * (b < 12) + [("silu", b - 1)] * (1 <= b < 13) + [("c_turn", b - 2)] * (b >= 2)
    out += [("gate_in",), ("decay",)] + [("qk_turn", t) for t in range(NT)]
    tokens = [("token", c, t) for c in (3, 2, 0, 1) for t in range(NT)]
    out += flat(weave(alone(deltanet(0)), alone(tokens)))
    out += [("first_states",), ("rope", 1), ("rope", 2)]
    rest = [("da_turn", t) for t in range(NT)] + [("lam",)]
    rest = alone(rest + [("mod", 4), ("mod", 5)] + [("gate", 0, v, h) for v in range(2) for h in range(2)])
    rest += parts(attention(0)) + alone([("mod", m) for m in range(6, 10)] + [("scales", 1)])
    out += flat(weave(alone(deltanet(1)), rest))
    rest = alone([("mod", 10), ("mod", 11)]) + parts(output(0)) + alone([("gate", 1, 0, h) for h in range(2)])
    rest += parts(retrieval([0]))
    out += flat(weave(alone(deltanet(2)), rest))
    latent = []
    for t in (1, 2):
        latent += attention(t) + output(t)
    latent += [("gate", 1, 1, h) for h in range(2)] + [("last_gain",)] + retrieval([1, 2])
    out += flat(weave(alone([("peer", n) for n in range(NG)]), parts(latent)))
    return out + [("peer_end",)]


def has_state(t, d):
    return t > 0


def updates_state(t, d):
    return t != (1, 2)[1 - d]


def program(nc, counts, x, cst, msk, par, wch, wba, kcT, vc, s0, subk, uv, nout,
            y, o_ck, o_cv, o_sf, o_sb):
    f32, i32, u32, bf16 = mybir.dt.float32, mybir.dt.int32, mybir.dt.uint32, mybir.dt.bfloat16
    ALU, ACT, AX = mybir.AluOpType, mybir.ActivationFunctionType, mybir.AxisListType
    ctx = ExitStack()
    with ctx:
        def sb(name, shape, dt=f32):
            return ctx.enter_context(nc.sbuf_tensor(name, shape, dt))

        def sem(name):
            return ctx.enter_context(nc.semaphore(name))

        signals = {}

        def signal(name):
            signals[name] = Signal(sem(name), name, counts)
            return signals[name]

        K = sb("consts", [P, C_END])
        M = sb("masks", [P, 2 * LEVELS * P], mybir.dt.uint16)
        Q = sb("params", [P, Q_END])
        ident, upper, lower = K[:, C_ID:C_ID + P], K[:, C_UP:C_UP + P], K[:, C_LO:C_LO + P]
        tri = [upper, lower]
        nb = [K[:, C_NBF:C_NBF + P], K[:, C_NBB:C_NBB + P]]
        iota = K[:, C_IOTA:C_IOTA + 16]

        def level_mask(d, lv):
            o = (d * LEVELS + lv) * P
            return M[:, o:o + P].bitcast(bf16)

        xs = sb("xs", [P, NT, D])
        hT = sb("hT", [P, NT, KD, P])
        tok = sb("tok", [P, NT, 1536])
        h2 = tok[:, :, 0:D]
        gate = sb("gate", [P, 2, D])
        wring = sb("wring", [P, WSLOTS, KD, CH])
        skr = sb("skr", [P, 512])
        diag = sb("diag", [P, GR * GU, P])
        modT = sb("modT", [P, 48, 2])
        scl = sb("scl", [P, 2, KD, 2])
        xo = sb("xo", [P, 2, D])
        ocat, oT = xo[:, 0, :], xo[:, 1, :]
        sq = sb("sq", [P, 512])
        small = sb("small", [P, 520])

        dn_tok = sb("dn_tok", [P, NT, 1536])
        z = sb("z", [P, NT, 512])
        ops = sb("ops", [P, 4096])
        qTa = ops[:, 0:1536].rearrange("p (h n) -> p h n", h=DA_H)
        vca = ops[:, 1536:2048]
        kTa = ops[:, 2048:4096].rearrange("p (h n) -> p h n", h=DA_H)
        E = sb("E", [P, 2, 2, 3 * P])
        aT = sb("aT", [P, 3 * P])

        big = sb("big", [P, GR * GU * 2 * D])
        rows = big[:, :].rearrange("p (s w) -> p s w", w=2 * D)
        pre = big[:, 0:1170].rearrange("p (s n) -> p s n", s=3)
        cy = big[:, 1176:2334].rearrange("p (s n) -> p s n", s=3)
        cz = big[:, 2336:3494].rearrange("p (s n) -> p s n", s=3)
        cjunk = big[:, 3584:3712]
        wb = big[:, 3712:3840].rearrange("p (k c) -> p k c", k=KD)

        def heads(ap):
            return ap.rearrange("p (h n) -> p h n", h=4)

        EG, DT, LT, TM, TT, PM, VB, KBG = [
            [big[:, (d * 8 + i) * 512:(d * 8 + i + 1) * 512] for d in range(2)] for i in range(8)]
        KDK = LT
        dqT = big[:, 8192:9728].rearrange("p (t c) -> p t c", t=NT)
        dkT = big[:, 9728:11264].rearrange("p (t c) -> p t c", t=NT)
        S = big[:, 11264:12288].rearrange("p (d c) -> p d c", d=2)

        spare = hT[:, 1:3].rearrange("p t k n -> p (t k n)")

        def sco(t, hh):
            return (tok[:, 1 + hh, 0:1024], ops[:, 2048 + 1024 * hh:3072 + 1024 * hh],
                    ops[:, 1024 * hh:1024 * hh + 1024])[t]

        def pqT(t, n):
            return spare[:, 1424:1936] if t == 0 else dn_tok[:, 1, 512 + 512 * (n % 2):1024 + 512 * (n % 2)]

        firsts = [spare[:, 0:512], dn_tok[:, 0, 0:512], dn_tok[:, 2, 512:1024]]
        seconds = [spare[:, 512:1424]] + [dn_tok[:, 0, 512:1424]] * 2
        sv = [f[:, 0:256] for f in firsts]
        siu = [f[:, 256:512].bitcast(u32) for f in firsts]
        e01 = [f[:, 256:512] for f in firsts]
        sif = [f[:, 0:256] for f in seconds]
        phf = [f[:, 256:512] for f in seconds]
        phl = [f[:, 256:512].bitcast(u32) for f in seconds]
        sv2 = [f[:, 512:640] for f in seconds]
        gex = [f[:, 640:768] for f in seconds]
        pos = [f[:, 768:896].bitcast(u32) for f in seconds]
        gsm = [f[:, 896:912] for f in seconds]

        idx = sb("idx", [P, NT, SLOTS], i32)
        gates = sb("gates", [P, NT, SLOTS])
        cur = sb("cur", [P, GR, GU], i32)
        dots = sb("dots", [P, GR, GU])
        gel = sb("gel", [P, GR, GU])

        used = [0]

        def sm(n):
            used[0] += n
            assert used[0] <= 520
            return small[:, used[0] - n:used[0]]

        def by_tile(ap):
            return ap.rearrange("p (t c) -> p t c", t=NT)

        cs, ssq, rst = sm(16), sm(6), sm(6)
        ssk, rnk = sm(24), sm(24)
        ba = by_tile(sm(48))
        beta, gg, g1, g2, gc, eg, bg = [by_tile(sm(24)) for _ in range(7)]
        nea, last, kds, kde = sm(8), sm(8), sm(8), sm(8)
        mx, nmx, zz, rz = sm(8), sm(8), sm(8), sm(8)
        lamv, lam = sm(4), sm(2)
        ob, obr = sm(4), sm(4)
        sub08 = Q[:, Q_SUB:Q_SUB + P]
        fss, fr = sm(1), sm(1)

        bank = [ctx.enter_context(nc.psum_tensor(f"bank{i}", [P, 512], f32)) for i in range(8)]
        acc = bank[0:2]

        def ps(*job):
            return bank[RING0 + counts.jobs.get(job, 0) % RINGN]

        chunk_in = [sem(f"chunk_in{i}") for i in range(WSLOTS)]
        params_in, consts_in, x_in, kv_in, s0_in, nout_in = [
            sem(n) for n in ("params_in", "consts_in", "x_in", "kv_in", "s0_in", "nout_in")]
        cache_out, state_out, y_out = sem("cache_out"), sem("state_out"), sem("y_out")
        product = signal("product")
        sk_in = sem("sk_in")
        c_silu, squares, rstd_in, rstd_out, xn_ready, hT_ready, mod_ready, scl_ready, gateb, gate_ready = [
            signal(n) for n in ("c_silu", "squares", "rstd_in", "rstd_out", "xn_ready", "hT_ready", "mod_ready",
                                "scl_ready", "gateb", "gate_ready")]
        pads, pre_ready, conv_ready, silu_ready, ctok_ready, knorm_in, knorm_out, kscaled = [
            signal(n) for n in ("pads", "pre_ready", "conv_ready", "silu_ready", "ctok_ready", "knorm_in",
                                "knorm_out", "kscaled")]
        ba_ready, beta_ready, softplus_in, softplus_out, g_ready, gc_ready, eg_ready, bg_ready = [
            signal(n) for n in ("ba_ready", "beta_ready", "softplus_in", "softplus_out", "g_ready", "gc_ready",
                                "eg_ready", "bg_ready")]
        qkT_ready, tok_ready, roped, daT_ready = [
            signal(n) for n in ("qkT_ready", "tok_ready", "roped", "daT_ready")]
        bc_ready, egrow_ready, kde_ready, dd_ready, dt_ready, kds_ready, lt_ready, at_ready = [
            signal(n) for n in ("bc_ready", "egrow_ready", "kde_ready", "dd_ready", "dt_ready", "kds_ready",
                                "lt_ready", "at_ready")]
        dn_pool, p_ready, t_ready, nw_ready, vn_ready, osum_ready, s_ready = [
            signal(n) for n in ("dn_pool", "p_ready", "t_ready", "nw_ready", "vn_ready", "osum_ready", "s_ready")]
        lam_in, lam_exp, mx_ready, e_ready, a_ready, aT_ready, av_ready = [
            signal(n) for n in ("lam_in", "lam_exp", "mx_ready", "e_ready", "a_ready", "aT_ready", "av_ready")]
        on_in, on_out, ocat_ready, oT_ready, x2_ready, h2_ready = [
            signal(n) for n in ("on_in", "on_out", "ocat_ready", "oT_ready", "x2_ready", "h2_ready")]
        pq_ready, sco_ready, gx_in, gx_out, idx_ready = [
            signal(n) for n in ("pq_ready", "sco_ready", "gx_in", "gx_out", "idx_ready")]
        rows_in = [sem(f"rows_in{r}") for r in range(GR)]
        gather_go = sem("gather_go")
        cur_ready, dot_ready, gelu_ready, diag_ready, vsum_done = [
            sem(n) for n in ("cur_ready", "dot_ready", "gelu_ready", "diag_ready", "vsum_done")]
        acc_done, acc_read, y_ready, fin_in, fin_out = [
            signal(n) for n in ("acc_done", "acc_read", "y_ready", "fin_in", "fin_out")]
        dve_step, act_step, pool_step = sem("dve_step"), sem("act_step"), sem("pool_step")

        def linker(eng, step):
            n = [0]

            def link(ins):
                n[0] += 1
                ins.then_inc(step, 1)
                eng.wait_ge(step, n[0])
            return link

        def reads(sig, key, *job):
            counts.release[job] = (sig.name, key)
            return sig.next(*key)

        def chunk(*name):
            return wring[:, CHUNK_NO[name] % WSLOTS]

        def chunk_here(*name):
            n = CHUNK_NO[name]
            return chunk_in[n % WSLOTS], 16 * (n // WSLOTS + 1)

        def col(ap, n):
            return ap.unsqueeze(2).to_broadcast([P, ap.shape[1], n])

        def rep(ap, n):
            return ap.unsqueeze(1).to_broadcast([P, n, ap.shape[1]])

        block = ctx.enter_context(nc.Block())
        STEPS = schedule()
        last_use = {("mod", m, 0): ("mod", m) for m in range(12)}
        last_use.update({("dn", i, 0): ("chT", 4 * i + 3) for i in range(3)})
        last_use.update({("z", 0, 0): ("tok", 3, 2)})
        last_use.update({("da", c, 0): ("tok", c, 2) for c in range(3)})
        last_use.update({("out", h, ps): ("wo", 2 * ps, h) for h in range(2) for ps in range(2)})
        last_use.update({("pq", i, ps): ("pq", i, 2 * ps) for i in range(4) for ps in range(2)})

        def run(parts):
            for step in STEPS:
                if step[0] in parts:
                    parts[step[0]](*step[1:])

        @block.sync
        def _(sp):
            sp.dma_start(Q[:, :], par).then_inc(params_in, 16)
            sp.dma_start(xs[:, :, :], x).then_inc(x_in, 16)
            for n, name in enumerate(CHUNKS):
                if n >= WSLOTS:
                    sp.wait_ge(*product.at(*last_use[CHUNKS[n - WSLOTS]]))
                src = STORED.index(name[:2] + (0,))
                sp.dma_start(wring[:, n % WSLOTS], wch[src]).then_inc(chunk_in[n % WSLOTS], 16)
                if n == 1:
                    sp.dma_start(K[:, :], cst).then_inc(consts_in, 16)
                    sp.dma_start(wb[:, :, :], wba).then_inc(consts_in, 16)
                if n == 5:
                    sp.dma_start(kTa[:, :, P:2 * P], kcT).then_inc(kv_in, 16)
                    sp.dma_start(vca, vc).then_inc(kv_in, 16)
                    sp.dma_start(M[:, :], msk).then_inc(kv_in, 16)
                if name[0] == "pq":
                    _, i, again = name
                    if i or again:
                        sp.wait_ge(*product.at("s", (i - 1) % 4, 2 * again if i else 0))
                    sp.dma_start(skr[:, :], subk[i]).then_inc(sk_in, 16)
            sp.wait_ge(*squares.at(1, 2))
            sp.wait_ge(*product.at("xT", 1, 2, 1))
            sp.dma_start(xo[:, 1, :], nout).then_inc(nout_in, 16)
            for t in range(NT):
                sp.wait_ge(*y_ready.at(t))
                sp.dma_start(y[t], xs[:, t, :]).then_inc(y_out, 16)
            sp.wait_ge(y_out, 16 * NT)
            sp.wait_ge(cache_out, 32)
            sp.wait_ge(state_out, 32)

        @block.gpsimd
        def _(pool):
            link = linker(pool, pool_step)
            nc.gpsimd.memset(pre[:, :, :], 0.0).then_inc(*pads.next())

            def token(c, t):
                if (c, t) == (1, 0):
                    pool.wait_ge(*tok_ready.at(1, 0))
                    pool.dma_start(o_ck, tok[:, 0, 512:1024]).then_inc(cache_out, 16)
                    pool.dma_start(o_cv, tok[:, 0, 1024:1536]).then_inc(cache_out, 16)

            def rope(t):
                if t == 1:
                    pool.wait_ge(consts_in, 32)
                    pool.wait_ge(*product.at("xT", 0, 2, 1))
                pool.wait_ge(*tok_ready.at(1, t))
                rt = xo[:, :, :].rearrange("p a (b n) -> p (a b) n", b=2)

                def table(c):
                    v = K[:, c + (t - 1) * 32:c + t * 32].rearrange("p (a f) -> p a f", a=2)
                    return v.unsqueeze(1).to_broadcast([P, 16, 2, 16])

                def half(i):
                    v = tok[:, t, 0:1024].rearrange("p (h a i f) -> p h a i f", h=16, a=2, i=2)
                    return v[:, :, :, i, :]

                tv = [rt[:, i, :].rearrange("p (h a f) -> p h a f", h=16, a=2) for i in range(4)]
                nc.gpsimd.tensor_tensor(tv[0], half(0), table(C_COS), ALU.mult)
                nc.gpsimd.tensor_tensor(tv[1], half(1), table(C_SIN), ALU.mult)
                nc.gpsimd.tensor_tensor(tv[2], half(1), table(C_COS), ALU.mult)
                link(nc.gpsimd.tensor_tensor(tv[3], half(0), table(C_SIN), ALU.mult))
                nc.gpsimd.tensor_tensor(half(0), tv[0], tv[1], ALU.subtract)
                nc.gpsimd.tensor_tensor(half(1), tv[2], tv[3], ALU.add).then_inc(*roped.next(t))
                pool.wait_ge(*roped.at(t))

            def dn_scale(pi):
                for t, d in PAIRS[pi]:
                    k4, v4 = heads(dn_tok[:, t, 512:1024]), heads(dn_tok[:, t, 1024:1536])
                    c4 = slice(4 * d, 4 * d + 4)
                    if pi == 0:
                        pool.wait_ge(*kscaled.at(2))
                        pool.wait_ge(*ctok_ready.at(11))
                        pool.wait_ge(*bg_ready.at())
                    else:
                        pool.wait_ge(*vn_ready.at(*PAIRS[pi - 1][d]))
                    nc.gpsimd.tensor_tensor(heads(VB[d]), v4, col(beta[:, t, c4], P), ALU.mult
                                            ).then_inc(*dn_pool.next("vb", t, d))
                    nc.gpsimd.tensor_tensor(heads(KBG[d]), k4, col(bg[:, t, c4], P), ALU.mult
                                            ).then_inc(*dn_pool.next("kbg", t, d))

            def dn_decay(pi):
                for t, d in PAIRS[pi]:
                    c4 = slice(4 * d, 4 * d + 4)
                    edge = P - 1 if d == 0 else 0
                    pool.wait_ge(*egrow_ready.at(t, d))
                    if pi == 2:
                        pool.wait_ge(*s_ready.at(*PAIRS[1][d]))
                    nc.gpsimd.tensor_copy(last[:, c4], heads(EG[d])[:, :, edge]).then_inc(*dn_pool.next("last", t, d))
                    pool.wait_ge(*dn_pool.at("last", t, d))
                    pool.wait_ge(*qkT_ready.at(t, 0))
                    nc.gpsimd.tensor_tensor(EG[d], EG[d], dqT[:, t, :], ALU.mult).then_inc(*dn_pool.next("qg", t, d))

            def dn_w(pi):
                for t, d in PAIRS[pi]:
                    if updates_state(t, d):
                        pool.wait_ge(*kds_ready.at(t, d))
                        pool.wait_ge(*product.at("P", t, d, LEVELS - 1))
                        nc.gpsimd.tensor_tensor(heads(KDK[d]), heads(dn_tok[:, t, 512:1024]),
                                                col(kds[:, 4 * d:4 * d + 4], P), ALU.mult
                                                ).then_inc(*dn_pool.next("kd", t, d))

            def first_states():
                for d in range(2):
                    pool.wait_ge(*s_ready.at(0, d))
                    pool.dma_start((o_sf, o_sb)[d], S[:, d, :]).then_inc(state_out, 16)
                pool.wait_ge(state_out, 32)
                pool.dma_start(S[:, :, :], s0).then_inc(s0_in, 16)

            def gather(t, n, g, r, held):
                if held:
                    pool.wait_ge(vsum_done, g - (GR - 1))
                nc.gpsimd.tensor_copy(cur[:, r, :], idx[:, t, bass.ds(n * GU, GU)]).then_inc(cur_ready, 1)
                pool.wait_ge(cur_ready, g + 1)
                pool.sem_inc(gather_go, 1)
                for u in range(GU):
                    nc.gpsimd.indirect_dma_start(
                        rows[:, r * GU + u, :], None, uv,
                        bass.IndirectOffsetOnAxis(ap=cur[:, r, u:u + 1], axis=0)).then_inc(rows_in[r], 16)

            def peer(n):
                if n == 0:
                    pool.wait_ge(*idx_ready.at(0))
                gather(0, n, n, n % GR, n >= GR)

            run({"token": token, "rope": rope, "dn_scale": dn_scale, "dn_decay": dn_decay, "dn_w": dn_w,
                 "first_states": first_states, "peer": peer})
            for t in (1, 2):
                g0 = t * NG
                pool.wait_ge(*idx_ready.at(t))
                gather(t, 0, g0, g0 % GR, True)
                with pool.Fori(0, ROUNDS) as i:
                    for r in range(GR):
                        gather(t, i * GR + (1 + r), i * GR + (g0 + 1 + r), (g0 + 1 + r) % GR, True)
                for n in REST:
                    gather(t, n, g0 + n, (g0 + n) % GR, True)

        @block.scalar
        def _(act):
            link = linker(act, act_step)

            def evac(out, job, sig, key, func=ACT.Copy, n=512, src=None, **kw):
                act.wait_ge(*product.at(*job))
                nc.scalar.activation(out, ps(*job)[:, 0:n] if src is None else src, func, **kw
                                     ).then_inc(*reads(sig, key, *job))

            act.wait_ge(params_in, 16)
            nc.scalar.activation(cs, Q[:, Q_C:Q_C + 16], ACT.Silu).then_inc(*c_silu.next())
            act.wait_ge(x_in, 16)

            def norm(w, t):
                if w:
                    act.wait_ge(*x2_ready.at(t, 1))
                c = slice(3 * w + t, 3 * w + t + 1)
                nc.scalar.activation(xo[:, 1, :], xs[:, t, :], ACT.Square, accum_out=ssq[:, c]
                                     ).then_inc(*squares.next(w, t))
                act.wait_ge(*rstd_in.at(w, t))
                nc.scalar.activation(rst[:, c], ssq[:, c], ACT.Sqrt).then_inc(*rstd_out.next(w, t))

            def x_copy(w, t):
                v = min(t, 1)
                act.wait_ge(*scl_ready.at(w))
                for h in range(2):
                    job = ("xT", w, t, h)
                    act.wait_ge(*product.at(*job))
                    for i in range(4):
                        k = 4 * h + i
                        ins = nc.scalar.activation(hT[:, t, k, :], ps(*job)[:, i * P:(i + 1) * P],
                                                   ACT.Identity, bias=modT[:, 24 * w + k, v:v + 1],
                                                   scale=scl[:, w, k, v:v + 1])
                    ins.then_inc(*reads(hT_ready, (w, t, h), *job))

            def channels(b):
                job = ("chT", b)
                act.wait_ge(*product.at(*job))
                if b == 0:
                    act.wait_ge(*pads.at())
                if b >= 3:
                    act.wait_ge(*conv_ready.at(b - 3))
                nc.scalar.activation(pre[:, b % 3, 2:130], ps(*job)[:, 0:P], ACT.Copy)
                nc.scalar.activation(pre[:, b % 3, 132:388], ps(*job)[:, P:T], ACT.Copy
                                     ).then_inc(*reads(pre_ready, (b,), *job))

            def silu(b):
                act.wait_ge(*conv_ready.at(b))
                if b >= 3:
                    act.wait_ge(*product.at("cT", b - 3))
                nc.scalar.activation(cz[:, b % 3, :], cy[:, b % 3, :], ACT.Silu).then_inc(*silu_ready.next(b))

            def c_turn(c):
                job = ("cT", c)
                act.wait_ge(*product.at(*job))
                v = ps(*job)[:, 0:T].rearrange("p (t n) -> p t n", t=NT)
                if c < 8:
                    for t in range(NT):
                        link(nc.scalar.activation(cjunk, v[:, t, :], ACT.Square,
                                                  accum_out=ssk[:, 8 * t + c:8 * t + c + 1]))
                nc.scalar.activation(dn_tok[:, :, c * P:(c + 1) * P], v, ACT.Copy
                                     ).then_inc(*reads(ctok_ready, (c,), *job))

            def gate_in():
                for t in range(NT):
                    evac(ba[:, t, :], ("ba", t), ba_ready, (t,), n=16)
                act.wait_ge(*ba_ready.at(2))
                nc.scalar.activation(beta[:, :, :], ba[:, :, 0:8], ACT.Sigmoid).then_inc(*beta_ready.next())
                act.wait_ge(*knorm_in.at())
                nc.scalar.activation(rnk, ssk, ACT.Sqrt).then_inc(*knorm_out.next())
                act.wait_ge(*softplus_in.at())
                link(nc.scalar.activation(g1[:, :, :], g1[:, :, :], ACT.Exp))
                link(nc.scalar.activation(g1[:, :, :], g1[:, :, :], ACT.Ln, bias=1.0))
                nc.scalar.activation(nea, Q[:, Q_ALOG:Q_ALOG + 8], ACT.Exp).then_inc(*softplus_out.next())

            def decay():
                for t in range(NT):
                    evac(gc[:, t, :], ("gc", t), gc_ready, (t,), n=8)
                act.wait_ge(*gc_ready.at(2))
                nc.scalar.activation(eg[:, :, :], gc[:, :, :], ACT.Exp).then_inc(*eg_ready.next())

            def qk_turn(t):
                for w in range(2):
                    evac((dqT, dkT)[w][:, t, :], ("qkT", t, w), qkT_ready, (t, w))

            def token(c, t):
                if c == 3:
                    evac(z[:, t, :], ("tok", c, t), tok_ready, (c, t), func=ACT.Silu)
                else:
                    evac(tok[:, t, c * 512:(c + 1) * 512], ("tok", c, t), tok_ready, (c, t))

            def da_turn(t):
                if t == 0:
                    act.wait_ge(kv_in, 48)
                for w in range(2):
                    o = t * P if w == 0 else (0, 2 * P, 3 * P)[t]
                    job = ("daT", t, w)
                    evac((qTa, kTa)[w][:, :, o:o + P], job, daT_ready, (t, w), src=heads(ps(*job)[:, :]))

            def gate_rows(w, v, h):
                if w:
                    act.wait_ge(*x2_ready.at(2 * v, 1))
                evac(gate[:, v, h * 512:(h + 1) * 512], ("gate", w, v, h), gate_ready, (w, v, h))

            def lam_step():
                act.wait_ge(*lam_in.at())
                nc.scalar.activation(lamv[:, 2:4], lamv[:, 0:2], ACT.Exp).then_inc(*lam_exp.next())

            def dn_decay(pi):
                for t, d in PAIRS[pi]:
                    job = ("gr", t, d)
                    act.wait_ge(*product.at(*job))
                    if pi:
                        act.wait_ge(*dn_pool.at("qg", *PAIRS[pi - 1][d]))
                        act.wait_ge(*product.at("o", *PAIRS[pi - 1][d]))
                    else:
                        act.wait_ge(*product.at("cT", 11))
                        act.wait_ge(*ctok_ready.at(11))
                    nc.scalar.activation(EG[d], ps(*job)[:, :], ACT.Exp).then_inc(*egrow_ready.next(t, d))
                for t, d in PAIRS[pi]:
                    c4 = slice(4 * d, 4 * d + 4)
                    act.wait_ge(*kde_ready.at(t, d))
                    if pi:
                        act.wait_ge(*dn_pool.at("kd", *PAIRS[pi - 1][d]))
                    nc.scalar.activation(kds[:, c4], kde[:, c4], ACT.Exp).then_inc(*kds_ready.next(t, d))
                    act.wait_ge(*dd_ready.at(t, d))
                    nc.scalar.activation(DT[d], DT[d], ACT.Exp).then_inc(*dt_ready.next(t, d))

            def dn_w(pi):
                for t, d in PAIRS[pi]:
                    if has_state(t, d):
                        evac(PM[d], ("wT", t, d), nw_ready, (t, d), scale=-1.0)

            def expo(t, h):
                nk = P if t == 0 else 3 * P
                n = t * DA_H + h
                act.wait_ge(*mx_ready.at(t, h))
                if n >= 2:
                    act.wait_ge(*product.at("aT", *divmod(n - 2, DA_H)))
                if h == 0 and t:
                    act.wait_ge(*a_ready.at(t - 1, 3))
                for m in range(2):
                    c = slice(2 * h + m, 2 * h + m + 1)
                    job = ("sc", t, 2 * h + m)
                    nc.scalar.activation(E[:, h % 2, m, 0:nk], ps(*job)[:, 0:nk], ACT.Exp,
                                         bias=nmx[:, c], scale=DA_DH ** -0.5, accum_out=zz[:, c]
                                         ).then_inc(*reads(e_ready, (t, 2 * h + m), *job))

            def a_copy(t, h):
                nk = P if t == 0 else 3 * P
                n = t * DA_H + h
                if n:
                    act.wait_ge(*product.at("av", *divmod(n - 1, DA_H)))
                evac(aT[:, 0:nk], ("aT", t, h), aT_ready, (t, h), n=nk)

            def head_norm(t, g):
                act.wait_ge(*on_in.at(t, g))
                nc.scalar.activation(obr, ob, ACT.Sqrt).then_inc(*on_out.next(t, g))

            def o_copy(t):
                for h in range(2):
                    evac(oT[:, h * 512:(h + 1) * 512], ("oT", t, h), oT_ready, (t, h))

            def h_copy(t):
                if t == 0:
                    act.wait_ge(cache_out, 32)
                for h in range(2):
                    evac(h2[:, t, h * 512:(h + 1) * 512], ("h2", t, h), h2_ready, (t, h))

            unit = [0]

            def q_copy(i, t):
                n = unit[0]
                unit[0] += 1
                before = retrieval_units.index((i, t)) - (1 if t == 0 else 2)
                if before >= 0:
                    act.wait_ge(*product.at("s", *retrieval_units[before]))
                evac(pqT(t, i * 2 + t), ("pq", i, t), pq_ready, (i, t))

            def s_copy(i, t):
                hh = i // 2
                o = 512 * (i % 2)
                evac(sco(t, hh)[:, o:o + 512], ("s", i, t), sco_ready, (i, t))

            def experts(t, hh):
                act.wait_ge(*gx_in.at(t, hh))
                g = gex[t][:, 64 * hh:64 * hh + 64]
                nc.scalar.activation(g, g, ACT.Exp).then_inc(*gx_out.next(t, hh))

            def gelu(g, r):
                act.wait_ge(dot_ready, g + 1)
                nc.scalar.activation(gel[:, r, :], dots[:, r, :], ACT.Gelu).then_inc(gelu_ready, 1)

            retrieval_units = [(i, 0) for i in range(4)] + [(i, t) for i in range(4) for t in (1, 2)]
            run({"norm": norm, "x_copy": x_copy, "channels": channels, "silu": silu, "c_turn": c_turn,
                 "gate_in": gate_in, "decay": decay, "qk_turn": qk_turn, "token": token, "da_turn": da_turn,
                 "gate": gate_rows, "lam": lam_step, "dn_decay": dn_decay, "dn_w": dn_w, "expo": expo,
                 "a_copy": a_copy, "head_norm": head_norm, "o_copy": o_copy, "h_copy": h_copy, "q_copy": q_copy,
                 "s_copy": s_copy, "experts": experts, "peer": lambda n: gelu(n, n % GR)})

            def last_root(t):
                act.wait_ge(*fin_in.at(t))
                nc.scalar.activation(fr, fss, ACT.Sqrt).then_inc(*fin_out.next(t))

            last_root(0)
            for t in (1, 2):
                g0 = t * NG
                gelu(g0, g0 % GR)
                with act.Fori(0, ROUNDS) as i:
                    for r in range(GR):
                        gelu(i * GR + (g0 + 1 + r), (g0 + 1 + r) % GR)
                for n in REST:
                    gelu(g0 + n, (g0 + n) % GR)
                last_root(t)

        @block.tensor
        def _(pe):
            order = []

            def begin(*job):
                n = len(order)
                counts.jobs[job] = n
                if n >= RINGN:
                    got = counts.release.get(order[n - RINGN])
                    if got:
                        pe.wait_ge(*signals[got[0]].at(*got[1]))
                order.append(job)
                return bank[RING0 + n % RINGN]

            def end(ins, *job):
                ins.then_inc(*product.next(*job))

            def mm(out, lhsT, rhs, first=True, last=True):
                return nc.tensor.matmul(out, lhsT, rhs, start=first, stop=last)

            def turn(src, *job, n=4):
                b = begin(*job)
                for i in range(n):
                    ins = nc.tensor.transpose(b[:, i * P:(i + 1) * P], src[:, i * P:(i + 1) * P], ident)
                end(ins, *job)

            def mod(m):
                if m == 0:
                    pe.wait_ge(*c_silu.at())
                pe.wait_ge(*chunk_here("mod", m, 0))
                b = begin("mod", m)
                w = chunk("mod", m, 0)
                for i in range(4):
                    for k in range(KD):
                        ins = mm(b[:, 2 * i:2 * i + 2], w[:, k, i * P:(i + 1) * P], cs[:, 2 * k:2 * k + 2],
                                 k == 0, k == KD - 1)
                end(ins, "mod", m)

            def x_turn(w, t):
                if (w, t) == (0, 0):
                    pe.wait_ge(consts_in, 32)
                pe.wait_ge(*xn_ready.at(w, t))
                for h in range(2):
                    turn(xo[:, 0, h * 512:(h + 1) * 512], "xT", w, t, h)

            def channels(c):
                if c == 0:
                    pe.wait_ge(*hT_ready.at(0, 2, 1))
                pe.wait_ge(*chunk_here("dn", c // 4, 0))
                b = begin("chT", c)
                w = chunk("dn", c // 4, 0)
                o = (c % 4) * P
                for k in range(KD):
                    ins = mm(b[:, 0:T].rearrange("p (t n) -> p t n", t=NT), w[:, k, o:o + P], hT[:, :, k, :],
                             k == 0, k == KD - 1)
                end(ins, "chT", c)

            def c_turn(c):
                pe.wait_ge(*silu_ready.at(c))
                b = begin("cT", c)
                for t in range(NT):
                    o = (0, 130, 258)[t]
                    ins = nc.tensor.transpose(b[:, t * P:(t + 1) * P], cz[:, c % 3, o:o + P], ident)
                end(ins, "cT", c)

            def gate_in():
                for t in range(NT):
                    b = begin("ba", t)
                    for k in range(KD):
                        ins = mm(b[:, 0:16], hT[:, t, k, :], wb[:, k, :], k == 0, k == KD - 1)
                    end(ins, "ba", t)

            def decay():
                pe.wait_ge(*g_ready.at())
                for t in range(NT):
                    b = begin("gc", t)
                    for d in range(2):
                        ins = mm(b[:, 4 * d:4 * d + 4], tri[d], gg[:, t, 4 * d:4 * d + 4])
                    end(ins, "gc", t)

            def qk_turn(t):
                pe.wait_ge(*kscaled.at(t))
                for w in range(2):
                    turn(dn_tok[:, t, w * 512:(w + 1) * 512], "qkT", t, w)

            def token(c, t):
                kind = ("da", c, 0) if c < 3 else ("z", 0, 0)
                pe.wait_ge(*chunk_here(*kind))
                b = begin("tok", c, t)
                for k in range(KD):
                    ins = mm(b[:, :], hT[:, t, k, :], chunk(*kind)[:, k, :], k == 0, k == KD - 1)
                end(ins, "tok", c, t)

            def da_turn(t):
                pe.wait_ge(*(roped.at(t) if t else tok_ready.at(1, 0)))
                for w in range(2):
                    turn(tok[:, t, w * 512:(w + 1) * 512], "daT", t, w)

            def gate_rows(w, v, h):
                pe.wait_ge(*gateb.at(w, v, h))
                turn(sq[:, :], "gate", w, v, h)

            def per_head(job, terms):
                b = begin(*job)
                for h in range(4):
                    s = slice(h * P, (h + 1) * P)
                    for i, (l, r) in enumerate(terms):
                        ins = mm(b[:, s], l[:, s], r[:, s], i == 0, i == len(terms) - 1)
                end(ins, *job)

            def dn_decay(pi):
                for t, d in PAIRS[pi]:
                    pe.wait_ge(*bc_ready.at("g", t, d))
                    b = begin("gr", t, d)
                    for h in range(4):
                        ins = mm(b[:, h * P:(h + 1) * P], LT[d][:, h * P:(h + 1) * P], tri[d])
                    end(ins, "gr", t, d)

            def dn_scores(pi):
                for t, d in PAIRS[pi]:
                    pe.wait_ge(*qkT_ready.at(t, 1))
                    per_head(("kk", t, d), [(dkT[:, t, :], dkT[:, t, :])])
                for t, d in PAIRS[pi]:
                    pe.wait_ge(*bc_ready.at("b", t, d))
                    turn(PM[d], "br", t, d)
                for t, d in PAIRS[pi]:
                    per_head(("qk", t, d), [(dkT[:, t, :], dqT[:, t, :])])

            def dn_p(pi, lv):
                for t, d in PAIRS[pi]:
                    if lv == 0:
                        pe.wait_ge(*lt_ready.at(t, d))
                        turn(LT[d], "P", t, d, 0)
                    else:
                        pe.wait_ge(*t_ready.at("T", t, d, lv - 1))
                        per_head(("P", t, d, lv), [(LT[d], TM[d])])

            def dn_t(pi, lv):
                for t, d in PAIRS[pi]:
                    pe.wait_ge(*p_ready.at(t, d, lv))
                    if lv == 0:
                        turn(PM[d], "TT", t, d, 0)
                    else:
                        pe.wait_ge(*t_ready.at("TT", t, d, lv - 1))
                        if lv < LEVELS - 1:
                            per_head(("T", t, d, lv), [(TT[d], PM[d])])
                        per_head(("TT", t, d, lv), [(PM[d], TT[d])])

            def dn_w(pi):
                for t, d in PAIRS[pi]:
                    if has_state(t, d):
                        pe.wait_ge(*t_ready.at("TT", t, d, LEVELS - 1))
                        pe.wait_ge(*dn_pool.at("kbg", t, d))
                        per_head(("wT", t, d), [(KBG[d], TT[d])])

            def dn_v(pi):
                for t, d in PAIRS[pi]:
                    pe.wait_ge(*t_ready.at("TT", t, d, LEVELS - 1))
                    pe.wait_ge(*dn_pool.at("vb", t, d))
                    if has_state(t, d):
                        pe.wait_ge(*nw_ready.at(t, d))
                        pe.wait_ge(s0_in, 16)
                        if pi == 2:
                            pe.wait_ge(*s_ready.at(*PAIRS[1][d]))
                        per_head(("vn", t, d), [(TT[d], VB[d]), (PM[d], S[:, d, :])])
                    else:
                        per_head(("vn", t, d), [(TT[d], VB[d])])

            def dn_o(pi):
                for t, d in PAIRS[pi]:
                    pe.wait_ge(*at_ready.at(t, d))
                    pe.wait_ge(*vn_ready.at(t, d))
                    pe.wait_ge(*dn_pool.at("qg", t, d))
                    terms = [(EG[d], S[:, d, :])] if has_state(t, d) else []
                    per_head(("o", t, d), terms + [(DT[d], TM[d])])

            def dn_s(pi):
                for t, d in PAIRS[pi]:
                    if updates_state(t, d):
                        pe.wait_ge(*dn_pool.at("kd", t, d))
                        per_head(("S", t, d), [(KDK[d], TM[d])])

            def score(t, h):
                nk, ko = (P, 0) if t == 0 else (3 * P, P)
                if t == 0 and h == 0:
                    pe.wait_ge(kv_in, 48)
                    pe.wait_ge(*daT_ready.at(2, 1))
                for m in range(2):
                    b = begin("sc", t, 2 * h + m)
                    s = slice(64 * m, 64 * m + 64)
                    ins = mm(b[:, 0:nk], qTa[s, h, t * P:(t + 1) * P], kTa[s, h, ko:ko + nk])
                    end(ins, "sc", t, 2 * h + m)

            def a_turn(t, h):
                pe.wait_ge(*a_ready.at(t, h))
                turn(E[:, h % 2, 0, :], "aT", t, h, n=1 if t == 0 else 3)

            def value(t, h):
                pe.wait_ge(*aT_ready.at(t, h))
                b = begin("av", t, h)
                s = slice(h * P, (h + 1) * P)
                s1 = slice(1024 + h * P, 1024 + (h + 1) * P)
                vals = [tok[:, 0, s1]] if t == 0 else [vca[:, s], tok[:, 1, s1], tok[:, 2, s1]]
                for j, v in enumerate(vals):
                    ins = mm(b[:, 0:P], aT[:, j * P:(j + 1) * P], v, j == 0, j == len(vals) - 1)
                end(ins, "av", t, h)

            def o_turn(t):
                pe.wait_ge(*ocat_ready.at(t, 1))
                for h in range(2):
                    turn(ocat[:, h * 512:(h + 1) * 512], "oT", t, h)

            def w_out(t, h):
                pe.wait_ge(*oT_ready.at(t, 1))
                name = ("out", h, min(t, 1))
                pe.wait_ge(*chunk_here(*name))
                b = begin("wo", t, h)
                for k in range(KD):
                    ins = mm(b[:, :], oT[:, k * P:(k + 1) * P], chunk(*name)[:, k, :], k == 0, k == KD - 1)
                end(ins, "wo", t, h)

            def h_turn(t):
                pe.wait_ge(*hT_ready.at(1, t, 1))
                for h in range(2):
                    turn(hT[:, t, 4 * h:4 * h + 4, :].rearrange("p k n -> p (k n)"), "h2", t, h)

            def query(i, t):
                name = ("pq", i, min(t, 1))
                pe.wait_ge(*chunk_here(*name))
                w = chunk(*name)
                b = begin("pq", i, t)
                for j in range(4):
                    for k in range(KD):
                        ins = mm(b[:, j * P:(j + 1) * P], w[:, k, j * P:(j + 1) * P], hT[:, t, k, :],
                                 k == 0, k == KD - 1)
                end(ins, "pq", i, t)

            def key_score(i, t):
                pe.wait_ge(sk_in, 16 * (4 * min(t, 1) + i + 1))
                pe.wait_ge(*pq_ready.at(i, t))
                q = pqT(t, i * 2 + t)
                b = begin("s", i, t)
                for j in range(4):
                    ins = mm(b[:, j * P:(j + 1) * P], q[:, j * P:(j + 1) * P], skr[:, j * P:(j + 1) * P])
                end(ins, "s", i, t)

            def v_sum(g, r, first=False, last=False):
                pe.wait_ge(diag_ready, g + 1)
                for u in range(GU):
                    for h in range(2):
                        ins = mm(acc[h][:, :], diag[:, r * GU + u, :],
                                 rows[:, r * GU + u, D + h * 512:D + (h + 1) * 512],
                                 first and u == 0, last and u == GU - 1)
                ins.then_inc(vsum_done, 1)

            def peer(n):
                if n:
                    v_sum(n - 1, (n - 1) % GR, n == 1)

            run({"mod": mod, "x_turn": x_turn, "channels": channels, "c_turn": c_turn, "gate_in": gate_in,
                 "decay": decay, "qk_turn": qk_turn, "token": token, "da_turn": da_turn, "gate": gate_rows,
                 "dn_decay": dn_decay, "dn_scores": dn_scores, "dn_p": dn_p, "dn_t": dn_t, "dn_w": dn_w,
                 "dn_v": dn_v, "dn_o": dn_o, "dn_s": dn_s, "score": score, "a_turn": a_turn, "value": value,
                 "o_turn": o_turn, "w_out": w_out, "h_turn": h_turn, "query": query, "key_score": key_score,
                 "peer": peer, "peer_end": lambda: v_sum(NG - 1, (NG - 1) % GR, False, True)})
            for t in (1, 2):
                g0 = t * NG
                pe.wait_ge(*acc_read.at(t - 1))
                v_sum(g0, g0 % GR, True)
                with pe.Fori(0, ROUNDS) as i:
                    for r in range(GR):
                        v_sum(i * GR + (g0 + 1 + r), (g0 + 1 + r) % GR)
                for n in REST:
                    v_sum(g0 + n, (g0 + n) % GR, False, n == NG - 1)

        @block.vector
        def _(dve):
            link = linker(dve, dve_step)
            V = nc.vector
            sq_reader = []

            def sq_free():
                if sq_reader:
                    dve.wait_ge(*product.at(*sq_reader.pop()))

            def norm(w, t):
                c = slice(3 * w + t, 3 * w + t + 1)
                dve.wait_ge(*squares.at(w, t))
                V.tensor_scalar(ssq[:, c], ssq[:, c], 1.0 / D, EPS, ALU.mult, ALU.add).then_inc(*rstd_in.next(w, t))
                dve.wait_ge(*rstd_out.at(w, t))
                link(V.reciprocal(rst[:, c], rst[:, c]))
                if t and not w:
                    dve.wait_ge(*product.at("xT", w, t - 1, 1))
                V.tensor_scalar(xo[:, 0, :], xs[:, t, :], rst[:, c], None, ALU.mult).then_inc(*xn_ready.next(w, t))

            def mod(m):
                job = ("mod", m)
                if m == 0:
                    dve.wait_ge(params_in, 16)
                dve.wait_ge(*product.at(*job))
                V.tensor_tensor(modT[:, 4 * m:4 * m + 4, :], ps(*job)[:, 0:8].rearrange("p (i v) -> p i v", v=2),
                                col(Q[:, Q_BMOD + 4 * m:Q_BMOD + 4 * m + 4], 2), ALU.add
                                ).then_inc(*reads(mod_ready, (m,), *job))

            def scales(w):
                dve.wait_ge(*mod_ready.at((3, 9)[w]))
                q = (Q_NA, Q_NF)[w]
                V.scalar_tensor_tensor(out=scl[:, w, :, :], in0=modT[:, 24 * w + 8:24 * w + 16, :], scalar=1.0,
                                       in1=col(Q[:, q:q + 8], 2), op0=ALU.add, op1=ALU.mult
                                       ).then_inc(*scl_ready.next(w))

            def channels(b):
                dve.wait_ge(*pre_ready.at(b))
                if b >= 3:
                    dve.wait_ge(*silu_ready.at(b - 3))
                o = cy[:, b % 3, :]
                for i in range(TAPS):
                    tap = Q[:, Q_CONV + TAPS * b + i:Q_CONV + TAPS * b + i + 1]
                    src = pre[:, b % 3, i:i + 386]
                    if i == 0:
                        link(V.tensor_scalar(o, src, tap, None, ALU.mult))
                    else:
                        ins = V.scalar_tensor_tensor(out=o, in0=src, scalar=tap, in1=o, op0=ALU.mult, op1=ALU.add)
                        if i < TAPS - 1:
                            link(ins)
                        else:
                            ins.then_inc(*conv_ready.next(b))

            def gate_in():
                dve.wait_ge(consts_in, 32)
                dve.wait_ge(*ba_ready.at(2))
                dve.wait_ge(*ctok_ready.at(7))
                V.tensor_scalar(ssk, ssk, EPS, None, ALU.add).then_inc(*knorm_in.next())
                link(V.tensor_tensor(g2[:, :, :], ba[:, :, 8:16], rep(Q[:, Q_DT:Q_DT + 8], NT), ALU.add))
                V.scalar_tensor_tensor(out=g1[:, :, :], in0=g2[:, :, :], scalar=-1.0, in1=g2[:, :, :],
                                       op0=ALU.mult, op1=ALU.min).then_inc(*softplus_in.next())
                dve.wait_ge(*knorm_out.at())
                link(V.reciprocal(rnk, rnk))
                rn = by_tile(rnk)
                link(V.tensor_scalar(rn[:, :, 0:4], rn[:, :, 0:4], P ** -0.5, None, ALU.mult))
                dve.wait_ge(*softplus_out.at())
                link(V.scalar_tensor_tensor(out=g1[:, :, :], in0=g2[:, :, :], scalar=0.0, in1=g1[:, :, :],
                                            op0=ALU.max, op1=ALU.add))
                V.scalar_tensor_tensor(out=gg[:, :, :], in0=g1[:, :, :], scalar=-1.0, in1=rep(nea, NT),
                                       op0=ALU.mult, op1=ALU.mult).then_inc(*g_ready.next())

            def decay():
                rn = by_tile(rnk)
                for t in range(NT):
                    v = dn_tok[:, t, 0:1024].rearrange("p (b n) -> p b n", n=P)
                    V.tensor_tensor(v, v, col(rn[:, t, :], P), ALU.mult).then_inc(*kscaled.next(t))
                dve.wait_ge(*eg_ready.at())
                dve.wait_ge(*beta_ready.at())
                V.tensor_tensor(bg[:, :, :], beta[:, :, :], eg[:, :, :], ALU.mult).then_inc(*bg_ready.next())

            def gate_rows(w, v, h):
                sq_free()
                o = (16, 40)[w] + 4 * h
                if (v, h) == (0, 0):
                    dve.wait_ge(*mod_ready.at((5, 11)[w]))
                V.tensor_copy(heads(sq[:, :]), col(modT[:, o:o + 4, v], P)).then_inc(*gateb.next(w, v, h))
                sq_reader.append(("gate", w, v, h))

            def lam_step():
                L = [Q[:, Q_LAM + 64 * i:Q_LAM + 64 * (i + 1)] for i in range(4)]
                sq_free()
                V.tensor_tensor_reduce(sq[:, 0:64], L[0], L[1], 1.0, 0.0, ALU.mult, ALU.add, lamv[:, 0:1])
                V.tensor_tensor_reduce(sq[:, 64:128], L[2], L[3], 1.0, 0.0, ALU.mult, ALU.add, lamv[:, 1:2]
                                       ).then_inc(*lam_in.next())
                V.tensor_scalar(sub08, Q[:, Q_SUB:Q_SUB + P], 1.0 - LAM_INIT, None, ALU.mult)
                dve.wait_ge(*lam_exp.at())
                link(V.tensor_scalar(lam[:, 0:1], lamv[:, 3:4], lamv[:, 2:3], -LAM_INIT, ALU.subtract, ALU.add))

            def dn_scale(pi):
                for t, d in PAIRS[pi]:
                    if pi == 0:
                        dve.wait_ge(*product.at("cT", 11))
                        dve.wait_ge(*ctok_ready.at(11))
                    else:
                        prev = PAIRS[pi - 1][d]
                        dve.wait_ge(*product.at("S", *prev))
                    V.tensor_copy(heads(LT[d]), col(gg[:, t, 4 * d:4 * d + 4], P)).then_inc(*bc_ready.next("g", t, d))
                    V.tensor_copy(heads(PM[d]), col(beta[:, t, 4 * d:4 * d + 4], P)).then_inc(*bc_ready.next("b", t, d))

            def dn_decay(pi):
                for t, d in PAIRS[pi]:
                    job = ("gr", t, d)
                    edge = P - 1 if d == 0 else 0
                    c4 = slice(4 * d, 4 * d + 4)
                    dve.wait_ge(*product.at(*job))
                    dve.wait_ge(*egrow_ready.at(t, d))
                    V.tensor_tensor(heads(DT[d]), heads(ps(*job)[:, :]), col(gc[:, t, c4], P), ALU.subtract)
                    if pi:
                        dve.wait_ge(*kds_ready.at(*PAIRS[pi - 1][d]))
                    V.tensor_tensor(kde[:, c4], heads(ps(*job)[:, :])[:, :, edge], gc[:, t, c4], ALU.subtract
                                    ).then_inc(*reads(kde_ready, (t, d), *job))
                    dve.wait_ge(*kde_ready.at(t, d))
                    V.tensor_tensor(heads(DT[d]), heads(DT[d]), rep(nb[d], 4), ALU.min).then_inc(*dd_ready.next(t, d))

            def dn_scores(pi):
                for t, d in PAIRS[pi]:
                    dve.wait_ge(*dt_ready.at(t, d))
                    dve.wait_ge(*product.at("kk", t, d))
                    V.tensor_tensor(LT[d], ps("kk", t, d)[:, :], DT[d], ALU.mult
                                    ).then_inc(*reads(lt_ready, ("k", t, d), "kk", t, d))
                for t, d in PAIRS[pi]:
                    dve.wait_ge(*product.at("br", t, d))
                    dve.wait_ge(*lt_ready.at("k", t, d))
                    V.scalar_tensor_tensor(out=LT[d], in0=ps("br", t, d)[:, :], scalar=-1.0, in1=LT[d],
                                           op0=ALU.mult, op1=ALU.mult).then_inc(*reads(lt_ready, (t, d), "br", t, d))
                for t, d in PAIRS[pi]:
                    dve.wait_ge(*product.at("qk", t, d))
                    V.tensor_tensor(DT[d], ps("qk", t, d)[:, :], DT[d], ALU.mult
                                    ).then_inc(*reads(at_ready, (t, d), "qk", t, d))

            def dn_p(pi, lv):
                if (pi, lv) == (0, 0):
                    dve.wait_ge(kv_in, 48)
                for t, d in PAIRS[pi]:
                    job = ("P", t, d, lv)
                    dve.wait_ge(*product.at(*job))
                    V.tensor_tensor(heads(PM[d]), heads(ps(*job)[:, :]), rep(level_mask(d, lv), 4), ALU.mult
                                    ).then_inc(*reads(p_ready, (t, d, lv), *job))

            def dn_t(pi, lv):
                for t, d in PAIRS[pi]:
                    if lv == 0:
                        dve.wait_ge(*p_ready.at(t, d, 0))
                        V.tensor_tensor(heads(TM[d]), heads(PM[d]), rep(ident, 4), ALU.add
                                        ).then_inc(*t_ready.next("T", t, d, 0))
                    elif lv < LEVELS - 1:
                        job = ("T", t, d, lv)
                        dve.wait_ge(*product.at(*job))
                        V.tensor_tensor(TM[d], ps(*job)[:, :], TM[d], ALU.add
                                        ).then_inc(*reads(t_ready, job, *job))
                    job = ("TT", t, d, lv)
                    dve.wait_ge(*product.at(*job))
                    if lv == 0:
                        V.tensor_tensor(heads(TT[d]), heads(ps(*job)[:, :]), rep(ident, 4), ALU.add
                                        ).then_inc(*reads(t_ready, job, *job))
                    else:
                        V.tensor_tensor(TT[d], ps(*job)[:, :], TT[d], ALU.add
                                        ).then_inc(*reads(t_ready, job, *job))

            def dn_v(pi):
                for t, d in PAIRS[pi]:
                    job = ("vn", t, d)
                    dve.wait_ge(*product.at(*job))
                    V.tensor_copy(TM[d], ps(*job)[:, :]).then_inc(*reads(vn_ready, (t, d), *job))

            def dn_o(pi):
                for t, d in PAIRS[pi]:
                    job = ("o", t, d)
                    dve.wait_ge(*product.at(*job))
                    out = dn_tok[:, t, 0:512]
                    if (t, d) in ((0, 0), (1, 0), (2, 1)):
                        V.tensor_copy(out, ps(*job)[:, :]).then_inc(*reads(osum_ready, (t, d), *job))
                    else:
                        if t == 0:
                            dve.wait_ge(*osum_ready.at(0, 0))
                        V.tensor_tensor(out, ps(*job)[:, :], out, ALU.add).then_inc(*reads(osum_ready, (t, d), *job))

            def dn_s(pi):
                for t, d in PAIRS[pi]:
                    if updates_state(t, d):
                        job = ("S", t, d)
                        dve.wait_ge(*product.at(*job))
                        if t == 0:
                            V.tensor_copy(S[:, d, :], ps(*job)[:, :]).then_inc(*reads(s_ready, (t, d), *job))
                        else:
                            dve.wait_ge(*dn_pool.at("last", t, d))
                            for h in range(4):
                                s = slice(h * P, (h + 1) * P)
                                ins = V.scalar_tensor_tensor(out=S[:, d, s], in0=S[:, d, s],
                                                             scalar=last[:, 4 * d + h:4 * d + h + 1],
                                                             in1=ps(*job)[:, s], op0=ALU.mult, op1=ALU.add)
                            ins.then_inc(*reads(s_ready, (t, d), *job))

            def expo(t, h):
                nk = P if t == 0 else 3 * P
                for m in range(2):
                    c = slice(2 * h + m, 2 * h + m + 1)
                    dve.wait_ge(*product.at("sc", t, 2 * h + m))
                    ins = V.tensor_reduce(mx[:, c], ps("sc", t, 2 * h + m)[:, 0:nk], AX.X, ALU.max)
                link(ins)
                V.tensor_scalar(nmx[:, 2 * h:2 * h + 2], mx[:, 2 * h:2 * h + 2], -DA_DH ** -0.5, None, ALU.mult
                                ).then_inc(*mx_ready.next(t, h))

            def diff(t, h):
                nk = P if t == 0 else 3 * P
                c, c1 = slice(2 * h, 2 * h + 1), slice(2 * h + 1, 2 * h + 2)
                dve.wait_ge(*e_ready.at(t, 2 * h + 1))
                link(V.reciprocal(rz[:, 2 * h:2 * h + 2], zz[:, 2 * h:2 * h + 2]))
                V.tensor_scalar(rz[:, c1], rz[:, c1], lam[:, 0:1], None, ALU.mult)
                link(V.tensor_scalar(E[:, h % 2, 0, 0:nk], E[:, h % 2, 0, 0:nk], rz[:, c], None, ALU.mult))
                V.scalar_tensor_tensor(out=E[:, h % 2, 0, 0:nk], in0=E[:, h % 2, 1, 0:nk], scalar=rz[:, c1],
                                       in1=E[:, h % 2, 0, 0:nk], op0=ALU.mult, op1=ALU.add
                                       ).then_inc(*a_ready.next(t, h))

            def v_copy(t, h):
                dve.wait_ge(*product.at("av", t, h))
                V.tensor_copy(ocat[:, h * P:(h + 1) * P], ps("av", t, h)[:, 0:P]
                              ).then_inc(*reads(av_ready, (t, h), "av", t, h))

            def head_norm(t, g):
                if g == 0:
                    dve.wait_ge(*av_ready.at(t, 3))
                    src = ocat[:, 0:512]
                else:
                    src = dn_tok[:, t, 0:512]
                    dve.wait_ge(*osum_ready.at(t, (1, 1, 0)[t]))
                    dve.wait_ge(*tok_ready.at(3, t))
                s4 = heads(src)
                sq_free()
                link(V.tensor_tensor(sq[:, :], src, src, ALU.mult))
                link(V.tensor_reduce(ob, heads(sq[:, :]), AX.X, ALU.add))
                V.tensor_scalar(ob, ob, 1.0 / P, EPS, ALU.mult, ALU.add).then_inc(*on_in.next(t, g))
                dve.wait_ge(*on_out.at(t, g))
                link(V.reciprocal(obr, obr))
                link(V.tensor_tensor(s4, s4, col(obr, P), ALU.mult))
                if g == 0:
                    V.tensor_tensor(s4, s4, rep(sub08, 4), ALU.mult).then_inc(*ocat_ready.next(t, 0))
                else:
                    link(V.tensor_tensor(s4, s4, rep(Q[:, Q_DNN:Q_DNN + P], 4), ALU.mult))
                    V.tensor_tensor(ocat[:, 512:1024], src, z[:, t, :], ALU.mult).then_inc(*ocat_ready.next(t, 1))

            def resid(t, h):
                v = min(t, 1)
                dve.wait_ge(*product.at("wo", t, h))
                dve.wait_ge(*gate_ready.at(0, v, h))
                s = slice(h * 512, (h + 1) * 512)
                sq_free()
                V.tensor_tensor(sq[:, :], ps("wo", t, h)[:, :], gate[:, v, s], ALU.mult
                                ).then_inc(*reads(x2_ready, ("g", t, h), "wo", t, h))
                dve.wait_ge(*x2_ready.at("g", t, h))
                V.tensor_tensor(xs[:, t, s], xs[:, t, s], sq[:, :], ALU.add).then_inc(*x2_ready.next(t, h))
                dve.wait_ge(*x2_ready.at(t, h))

            def two_rounds(src, vals, inds):
                for r in range(2):
                    o = slice(8 * r, 8 * r + 8)
                    for s, v in zip(src, vals):
                        ins = V.max(v[:, o], s)
                    link(ins)
                    for s, v, i in zip(src, vals, inds):
                        ins = V.max_index(i[:, o], v[:, o], s)
                    link(ins)
                    if r == 0:
                        for s, v in zip(src, vals):
                            ins = V.match_replace(s, v[:, o], s, NEG)
                        link(ins)

            def blocks(ap, n, first, count):
                return [ap[:, n * b:n * (b + 1)] for b in range(first, first + count)]

            def top_key(i, t):
                dve.wait_ge(*sco_ready.at(i, t))
                two_rounds(blocks(sco(t, i // 2), NKEY, 4 * (i % 2), 4), blocks(sv[t], TOPK, 4 * i, 4),
                           blocks(siu[t], TOPK, 4 * i, 4))

            def top_pair(t, hh):
                H = PEER_H // 2
                v4 = sv[t][:, 128 * hh:128 * hh + 128].rearrange("p (h i r) -> p h i r", h=H, i=2)
                c = sco(t, hh)
                link(V.tensor_tensor(c.rearrange("p (h a b) -> p h a b", h=H, a=TOPK),
                                     v4[:, :, 0, :].unsqueeze(3).to_broadcast([P, H, TOPK, TOPK]),
                                     v4[:, :, 1, :].unsqueeze(2).to_broadcast([P, H, TOPK, TOPK]), ALU.add))
                two_rounds(blocks(c, TOPK * TOPK, 0, H), blocks(sv2[t], TOPK, H * hh, H),
                           blocks(pos[t], TOPK, H * hh, H))

            def experts(t, hh):
                H = PEER_H // 2
                s = slice(64 * hh, 64 * hh + 64)
                s1 = slice(128 + 64 * hh, 128 + 64 * hh + 64)
                v2 = sv2[t][:, s].rearrange("p (h r) -> p h r", h=H)
                if hh == 0 and t:
                    dve.wait_ge(*gx_out.at(t - 1, 1))
                V.tensor_tensor(gex[t][:, s].rearrange("p (h r) -> p h r", h=H), v2,
                                v2[:, :, 0:1].to_broadcast([P, H, TOPK]), ALU.subtract).then_inc(*gx_in.next(t, hh))
                V.tensor_scalar(phl[t][:, s], pos[t][:, s], 4, None, ALU.logical_shift_right)
                link(V.tensor_scalar(phl[t][:, s1], pos[t][:, s], 15, None, ALU.bitwise_and))
                V.tensor_copy(phf[t][:, s], phl[t][:, s])
                V.tensor_copy(phf[t][:, s1], phl[t][:, s1])
                link(V.tensor_copy(sif[t][:, 128 * hh:128 * hh + 128], siu[t][:, 128 * hh:128 * hh + 128]))
                i4 = sif[t][:, 128 * hh:128 * hh + 128].rearrange("p (h i r) -> p h i r", h=H, i=2)
                c4 = sco(t, hh).rearrange("p (h a b) -> p h a b", h=H, a=TOPK)
                for w in range(2):
                    ph = phf[t][:, (s, s1)[w]].rearrange("p (h r) -> p h r", h=H)
                    link(V.tensor_tensor(c4, ph.unsqueeze(3).to_broadcast([P, H, TOPK, TOPK]),
                                         iota.unsqueeze(1).unsqueeze(1).to_broadcast([P, H, TOPK, TOPK]),
                                         ALU.is_equal))
                    link(V.tensor_tensor(c4, c4, i4[:, :, w, :].unsqueeze(2).to_broadcast([P, H, TOPK, TOPK]),
                                         ALU.mult))
                    o = e01[t][:, 128 * hh + 64 * w:128 * hh + 64 * w + 64]
                    link(V.tensor_reduce(o.rearrange("p (h r) -> p h r", h=H), c4, AX.X, ALU.add))
                a, b = e01[t][:, 128 * hh:128 * hh + 64], e01[t][:, 128 * hh + 64:128 * hh + 128]
                link(V.scalar_tensor_tensor(out=a, in0=a, scalar=float(NKEY), in1=b, op0=ALU.mult, op1=ALU.add))
                link(V.tensor_copy(idx[:, t, s], a))

            def slot_gates(t):
                g8 = gex[t].rearrange("p (h r) -> p h r", h=PEER_H)
                dve.wait_ge(*gx_out.at(t, 1))
                link(V.tensor_reduce(gsm[t][:, 0:8], g8, AX.X, ALU.add))
                link(V.reciprocal(gsm[t][:, 8:16], gsm[t][:, 0:8]))
                V.tensor_tensor(gates[:, t, :].rearrange("p (h r) -> p h r", h=PEER_H), g8,
                                col(gsm[t][:, 8:16], TOPK), ALU.mult).then_inc(*idx_ready.next(t))

            def dot_products(t, r, times):
                dve.wait_ge(rows_in[r], times * (16 * GU))
                for u in range(GU):
                    u_rows = rows[:, r * GU + u, 0:D]
                    ins = V.tensor_tensor_reduce(u_rows, u_rows, h2[:, t, :], 1.0, 0.0, ALU.mult, ALU.add,
                                                 dots[:, r, u:u + 1])
                ins.then_inc(dot_ready, 1)

            def diagonals(t, n, g, r):
                dve.wait_ge(gelu_ready, g + 1)
                for u in range(GU):
                    ins = V.tensor_scalar(diag[:, r * GU + u, :], ident, gel[:, r, u:u + 1],
                                          gates[:, t, bass.ds(n * GU + u, 1)], ALU.mult, ALU.mult)
                ins.then_inc(diag_ready, 1)

            def peer(n):
                if n == 0:
                    dve.wait_ge(*h2_ready.at(0, 1))
                dot_products(0, n % GR, n // GR + 1)
                if n:
                    diagonals(0, n - 1, n - 1, (n - 1) % GR)

            def last_norm(t):
                v = min(t, 1)
                dve.wait_ge(vsum_done, (t + 1) * NG)
                if t == 0:
                    dve.wait_ge(nout_in, 16)
                    dve.wait_ge(*gate_ready.at(1, 1, 1))
                    sq_free()
                for h in range(2):
                    s = slice(h * 512, (h + 1) * 512)
                    ins = V.tensor_tensor(sq[:, :], acc[h][:, :], gate[:, v, s], ALU.mult)
                    if h:
                        ins.then_inc(*acc_read.next(t))
                        dve.wait_ge(*acc_read.at(t))
                    else:
                        link(ins)
                    link(V.tensor_tensor(xs[:, t, s], xs[:, t, s], sq[:, :], ALU.add))
                link(V.tensor_tensor_reduce(xo[:, 0, :], xs[:, t, :], xs[:, t, :], 1.0, 0.0, ALU.mult, ALU.add, fss))
                V.tensor_scalar(fss, fss, 1.0 / D, EPS, ALU.mult, ALU.add).then_inc(*fin_in.next(t))
                dve.wait_ge(*fin_out.at(t))
                link(V.reciprocal(fr, fr))
                V.scalar_tensor_tensor(out=xs[:, t, :], in0=xs[:, t, :], scalar=fr, in1=xo[:, 1, :],
                                       op0=ALU.mult, op1=ALU.mult).then_inc(*y_ready.next(t))

            run({"norm": norm, "mod": mod, "scales": scales, "channels": channels, "gate_in": gate_in,
                 "decay": decay, "gate": gate_rows, "lam": lam_step, "dn_scale": dn_scale, "dn_decay": dn_decay,
                 "dn_scores": dn_scores, "dn_p": dn_p, "dn_t": dn_t, "dn_v": dn_v, "dn_o": dn_o, "dn_s": dn_s,
                 "expo": expo, "diff": diff, "v_copy": v_copy, "head_norm": head_norm, "resid": resid,
                 "top_key": top_key, "top_pair": top_pair, "experts": experts, "slot_gates": slot_gates,
                 "peer": peer, "peer_end": lambda: diagonals(0, NG - 1, NG - 1, (NG - 1) % GR)})
            last_norm(0)
            for t in (1, 2):
                g0 = t * NG
                dot_products(t, g0 % GR, g0 // GR + 1)
                with dve.Fori(0, ROUNDS) as i:
                    for r in range(GR):
                        dot_products(t, (g0 + 1 + r) % GR, i + ((g0 + 1 + r) // GR + 1))
                        diagonals(t, i * GR + r, i * GR + (g0 + r), (g0 + r) % GR)
                for n in REST:
                    dot_products(t, (g0 + n) % GR, (g0 + n) // GR + 1)
                    diagonals(t, n - 1, g0 + n - 1, (g0 + n - 1) % GR)
                diagonals(t, NG - 1, g0 + NG - 1, (g0 + NG - 1) % GR)
                last_norm(t)


_NAMES = ["x", "cst", "msk", "par", "wch", "wba", "kcT", "vc", "s0", "subk", "uv", "nout"]
_OUTS = [("y", (NT, P, D)), ("o_ck", (P, 512)), ("o_cv", (P, 512)), ("o_sf", (P, 512)), ("o_sb", (P, 512))]


def shape_constants():
    k = np.zeros((P, C_END), np.float32)
    i = np.arange(P)
    k[:, C_ID:C_ID + P] = np.eye(P)
    k[:, C_UP:C_UP + P] = i[:, None] <= i[None, :]
    k[:, C_LO:C_LO + P] = i[:, None] >= i[None, :]
    k[:, C_NBF:C_NBF + P] = np.where(i[None, :] >= i[:, None], 0.0, -BIG)
    k[:, C_NBB:C_NBB + P] = np.where(i[None, :] <= i[:, None], 0.0, -BIG)
    n = np.arange(2 * P)
    at = np.stack([n // GRID_W, n % GRID_W], -1).astype(np.float32)
    f = np.power(np.float32(10000.0), -np.arange(0, 32, 2, dtype=np.float32) / np.float32(32)).astype(np.float32)
    ang = (at[:, :, None] * f).astype(np.float32)
    for c, fn in ((C_COS, np.cos), (C_SIN, np.sin)):
        k[:, c:c + 64] = fn(ang).astype(np.float32).reshape(2, P, 32).transpose(1, 0, 2).reshape(P, 64)
    k[:, C_IOTA:C_IOTA + 16] = np.arange(16)
    return k


def level_masks():
    i = np.arange(P)
    out = []
    for lv in range(LEVELS):
        s = 1 << lv
        out.append((i[:, None] // (2 * s) == i[None, :] // (2 * s)) & (i[:, None] // s % 2 == 1)
                   & (i[None, :] // s % 2 == 0))
    return np.concatenate(out + [m.T for m in out], 1).astype(np.uint16) * np.uint16(BF16_ONE)


def _layout(a):
    def cols(v):
        return v.reshape(-1, P).T

    def rows(v):
        return np.broadcast_to(v.reshape(1, -1), (P, v.size))

    f = np.float32
    par = np.empty((P, Q_END), f)
    par[:, Q_C:Q_C + 16] = np.stack([cols(a["c_ctx"]), cols(a["c"][0])], -1).reshape(P, 16)
    par[:, Q_BMOD:Q_BMOD + 48] = cols(a["b_mod"][0])
    par[:, Q_NA:Q_NA + 8] = cols(a["norm_attn"][0])
    par[:, Q_NF:Q_NF + 8] = cols(a["norm_ffn"][0])
    par[:, Q_CONV:Q_CONV + 60] = a["conv_w"][0].reshape(TAPS, 12, P).transpose(2, 1, 0).reshape(P, 60)
    par[:, Q_DNN:Q_DNN + P] = rows(a["dn_norm"])
    par[:, Q_SUB:Q_SUB + P] = rows(a["subln"])
    par[:, Q_ALOG:Q_ALOG + 8] = rows(a["a_log"])
    par[:, Q_DT:Q_DT + 8] = rows(a["dt_bias"])
    for i, n in enumerate(("lambda_q1", "lambda_k1", "lambda_q2", "lambda_k2")):
        par[:, Q_LAM + 64 * i:Q_LAM + 64 * i + 64] = rows(a[n])
    w_in = a["w_in"][0]
    mats = {"mod": a["w_mod"][0], "da": w_in[:, 0:1536], "dn": w_in[:, 1536:3072], "z": w_in[:, 3072:3584],
            "out": a["w_out"][0], "pq": a["w_pq"][0]}
    wch = np.empty((len(STORED), P, KD, CH), f)
    for n, (kind, i, _) in enumerate(STORED):
        wch[n] = mats[kind][:, i * CH:(i + 1) * CH].reshape(KD, P, CH).transpose(1, 0, 2)
    uv = np.empty((a["expert_u"].shape[1], 2 * D), f)
    uv[:, :D] = a["expert_u"][0]
    uv[:, D:] = a["expert_v"][0]
    x = np.concatenate([a["x_prompt"][0], a["x_sample"][0]], 0).reshape(NT, P, D).transpose(1, 0, 2)
    s0 = np.stack([a["state_fwd"][0, 0], a["state_bwd"][0, 0]], 0)
    return {
        "x": x, "cst": shape_constants(), "msk": level_masks(), "par": par, "wch": wch,
        "wba": w_in[:, 3584:3600].reshape(KD, P, 16).transpose(1, 0, 2),
        "kcT": a["cache_k"][0, 0].reshape(P, DA_H, P).transpose(2, 1, 0),
        "vc": a["cache_v"][0, 0].reshape(P, 512),
        "s0": s0.transpose(2, 0, 1, 3).reshape(P, 2, 512),
        "subk": a["sub_keys"][0].reshape(4, 4, NKEY, P).transpose(0, 3, 1, 2).reshape(4, P, 512),
        "uv": uv, "nout": rows(a["norm_out"]),
    }


def kernel(**inputs):
    import concourse.bacc as _bacc
    from concourse.bass_utils import run_bass_kernel_spmd as _run

    a = {k: np.asarray(v) for k, v in inputs.items()}
    data = {k: np.ascontiguousarray(v) for k, v in _layout(a).items()}
    counts = Counts()
    for _ in range(2):
        nc = _bacc.Bacc("TRN2", target_bir_lowering=False, num_devices=1)
        args = [nc.dram_tensor(f"in_{n}", data[n].shape, mybir.dt.from_np(data[n].dtype), kind="ExternalInput").ap() for n in _NAMES]
        args += [nc.dram_tensor(f"out_{n}", s, mybir.dt.float32, kind="ExternalOutput").ap() for n, s in _OUTS]
        program(nc, counts, *args)
    r = _run(nc, [{f"in_{n}": data[n] for n in _NAMES}], core_ids=[0])
    got = {n: r.results[0][f"out_{n}"] for n, _ in _OUTS}
    y = got["y"].reshape(T, D)

    def state(s):
        return s.reshape(P, DN_H, P).transpose(1, 0, 2).reshape(1, 1, DN_H, P, P)

    return (y[:P].reshape(1, P, D), y[P:].reshape(1, 2 * P, D), got["o_ck"].reshape(1, 1, P, 2 * DA_H, DA_DH),
            got["o_cv"].reshape(1, 1, P, DA_H, 2 * DA_DH), state(got["o_sf"]), state(got["o_sb"]))
```

```python
import numpy as np
import concourse.bass as bass
from concourse import mybir
from contextlib import ExitStack

P = 128
D = 1024
KD = D // P
NT = 3
T = NT * P
DA_H, DA_DH = 4, 64
DN_H = 4
PEER_H, NKEY, TOPK = 8, 128, 16
SLOTS = PEER_H * TOPK
CH = 512
EPS = 1e-6
LAM_INIT = 0.2
GRID_W = 64
TAPS = 5
LEVELS = 7
BIG = 1e30
BF16_ONE = 0x3F80
NEG = -3.0e38

C_ID, C_UP, C_LO, C_NBF, C_NBB = 0, 128, 256, 384, 512
C_COS = 640
C_SIN = C_COS + 64
C_IOTA = C_SIN + 64
C_END = C_IOTA + 16
Q_C, Q_BMOD, Q_NA, Q_NF, Q_CONV = 0, 16, 64, 72, 80
Q_DNN, Q_SUB, Q_ALOG, Q_DT, Q_LAM = 140, 268, 396, 404, 412
Q_END = 668

CHUNKS = ([("mod", m, 0) for m in range(4)] + [("dn", i, 0) for i in range(3)] + [("da", c, 0) for c in range(3)]
          + [("z", 0, 0)]
          + [("mod", m, 0) for m in range(4, 10)]
          + [("out", 0, 0), ("out", 1, 0), ("mod", 10, 0), ("mod", 11, 0)] + [("pq", i, 0) for i in range(4)]
          + [("out", 0, 1), ("out", 1, 1)] + [("pq", i, 1) for i in range(4)])
CHUNK_NO = {c: n for n, c in enumerate(CHUNKS)}
STORED = [c for c in CHUNKS if c[2] == 0]
WSLOTS = 2

PAIRS = [[(0, 0), (0, 1)], [(1, 0), (2, 1)], [(2, 0), (1, 1)]]

GU = 1
GR = 6
NG = SLOTS // GU
LAG = 2
MIXED = 8 * GR
RING0, RINGN = 2, 6


def in_rounds(first, last):
    rounds = (last - first) // GR
    return rounds, range(first + rounds * GR, last)


class Counts:

    def __init__(self):
        self.at = {}
        self.jobs = {}
        self.release = {}


class Signal:

    def __init__(self, sem, name, counts):
        self.sem, self.name, self.counts, self.n = sem, name, counts, 0

    def next(self, *key):
        self.n += 1
        self.counts.at[(self.name,) + key] = self.n
        return self.sem, 1

    def at(self, *key):
        return self.sem, self.counts.at.get((self.name,) + key, 1)


WEIGHT = {"query": 4, "query_rest": 4, "w_out": 4, "w_out_rest": 4, "token": 8, "mod": 8, "top_pair": 4, "chosen": 4,
          "top_key": 5, "dn_t": 4, "dn_scores": 5, "dn_v": 4, "dn_o": 4, "dn_decay": 4, "head_norm": 4, "x_copy": 3,
          "slot_gates": 1, "experts": 1, "q_copy": 1, "s_copy": 1, "v_copy": 1, "a_copy": 1}


def weight(part):
    return sum(WEIGHT.get(step[0], 2) for step in part)


def weave(steps, between):
    out, n, done, placed = [], 0, 0, 0
    total, total2 = sum(map(weight, steps)), sum(map(weight, between))
    for s in steps:
        out.append(s)
        done += weight(s)
        while n < len(between) and placed * total < done * total2:
            out.append(between[n])
            placed += weight(between[n])
            n += 1
    return out + between[n:]


def deltanet(p):
    out = [("dn_scale", p), ("dn_decay", p), ("dn_scores", p)]
    for lv in range(LEVELS):
        out += [("dn_p", p, lv), ("dn_t", p, lv)]
    return out + [("dn_w", p), ("dn_v", p), ("dn_o", p), ("dn_s", p)]


def attention(t):
    out = []
    for k in range(DA_H + 2):
        for lag, names in ((2, ("a_copy",)), (0, ("score", "expo")), (2, ("value",)), (1, ("diff", "a_turn")),
                           (2, ("v_copy",))):
            if 0 <= k - lag < DA_H:
                out += [(n, t, k - lag) for n in names]
        out.append(("seam",))
    return out


def output(t):
    gap = [("seam",)] if t else []
    return ([("head_norm", t, 0), ("seam",), ("head_norm", t, 1), ("o_turn", t)] + gap + [("o_copy", t), ("seam",)]
            + [("w_out", t, 0), ("w_out_rest", t, 0)] + gap + [("w_out", t, 1), ("w_out_rest", t, 1), ("resid", t, 0)] + gap + [("resid", t, 1), ("norm", 1, t)]
            + [("seam",), ("x_turn", 1, t)] + gap + [("x_copy", 1, t), ("seam",), ("h_turn", t)] + gap
            + [("h_copy", t), ("seam",)])


def retrieval(units, now):
    out = []
    for k in range(len(units) + 3):
        for lag, names in ((0, ("query", "query_rest")), (1, ("q_copy", "key_score")), (2, ("s_copy",)), (3, ("top_key",))):
            if 0 <= k - lag < len(units):
                out += [(n,) + units[k - lag] for n in names if n != "top_key" or units[k - lag][1] in now]
        out.append(("seam",))
    return out


def choice(t, hh):
    return [("pair_sums", t, hh), ("top_pair", t, hh, 0), ("top_pair", t, hh, 1), ("places", t, hh),
            ("chosen", t, hh, 0), ("chosen", t, hh, 1), ("experts", t, hh), ("slot_gates", t, hh)]


def modulation(first, last):
    return [(name, m) for m in range(first, last) for name in ("mod", "mod_turn")]


def parts(steps):
    out, part = [], []
    for s in steps + [("seam",)]:
        if s[0] == "seam":
            out += [part] * bool(part)
            part = []
        else:
            part.append(s)
    return out


def alone(steps):
    return [[s] for s in steps]


def flat(lists):
    return [s for part in lists for s in part]


def schedule():
    out = []
    for t in range(NT):
        out += [("norm", 0, t), ("x_turn", 0, t), ("x_copy", 0, t)]
    out += modulation(0, 4) + [("scales", 0), ("modulate",)]
    for b in range(14):
        out += [("channels", b)] * (b < 12) + [("silu", b - 1)] * (1 <= b < 13) + [("c_turn", b - 2)] * (b >= 2)
    out += [("gate_in",)] + [("token", 0, t) for t in range(NT)] + [("decay",)] + [("qk_turn", t) for t in range(NT)]
    rest = alone([("token", 1, 0), ("token", 1, 1), ("rope", 1), ("token", 1, 2), ("rope", 2)])
    rest += alone([("token", 2, t) for t in range(NT)] + [("token", 3, t) for t in range(NT)])
    rest += alone([("da_turn", t) for t in range(NT)] + [("keep_qk",), ("lam",)])
    rest += parts(attention(0)) + alone(modulation(4, 6) + [("gate", 0, v, h) for v in range(2) for h in range(2)])
    out += flat(weave(alone(deltanet(0)), rest)) + [("first_states",)]
    rest = alone([("head_norm", 0, 0)] + modulation(6, 10) + [("scales", 1)])
    rest += parts(output(0)[2:]) + alone(modulation(10, 12))
    rest += parts(retrieval([(i, 0) for i in range(2)], (0,))) + alone(choice(0, 0))
    out += flat(weave(alone(deltanet(1)), rest))
    between = retrieval([(i, 0) for i in range(2, 4)], (0,)) + choice(0, 1)
    for step in deltanet(2):
        between += [step, ("seam",)]
    for t in (1, 2):
        between += attention(t) + output(t)
    between += [("gate", 1, v, h) for v in range(2) for h in range(2)]
    between += retrieval([(i, t) for i in range(4) for t in (1, 2)], (1,)) + choice(1, 0) + choice(1, 1)
    out += flat(weave(alone([("peer", 0, n) for n in range(SLOTS)]), alone(flat(parts(between)))))
    out += [("peer_end", 0), ("last_norm", 0)]
    between = []
    for i in range(4):
        between += [("top_key", i, 2), ("seam",)]
    between += choice(2, 0) + choice(2, 1)
    return out + flat(weave(alone([("peer", 1, n) for n in range(MIXED)]), alone(flat(parts(between)))))


def has_state(t, d):
    return t > 0


def updates_state(t, d):
    return t != (1, 2)[1 - d]


def program(nc, counts, x, cst, msk, par, wch, wba, kcT, vc, s0, subk, uv, nout,
            y, o_ck, o_cv, o_sf, o_sb):
    f32, i32, u32, bf16 = mybir.dt.float32, mybir.dt.int32, mybir.dt.uint32, mybir.dt.bfloat16
    ALU, ACT, AX = mybir.AluOpType, mybir.ActivationFunctionType, mybir.AxisListType
    ctx = ExitStack()
    with ctx:
        def sb(name, shape, dt=f32):
            return ctx.enter_context(nc.sbuf_tensor(name, shape, dt))

        def sem(name):
            return ctx.enter_context(nc.semaphore(name))

        signals = {}

        def signal(name):
            signals[name] = Signal(sem(name), name, counts)
            return signals[name]

        K = sb("consts", [P, C_END])
        M = sb("masks", [P, 2 * LEVELS * P], mybir.dt.uint16)
        Q = sb("params", [P, Q_END])
        ident, upper, lower = K[:, C_ID:C_ID + P], K[:, C_UP:C_UP + P], K[:, C_LO:C_LO + P]
        tri = [upper, lower]
        nb = [K[:, C_NBF:C_NBF + P], K[:, C_NBB:C_NBB + P]]
        iota = K[:, C_IOTA:C_IOTA + 16]

        def level_mask(d, lv):
            o = (d * LEVELS + lv) * P
            return M[:, o:o + P].bitcast(bf16)

        xs = sb("xs", [P, NT, D])
        hT = sb("hT", [P, NT, KD, P])
        tok = sb("tok", [P, NT, 1536])
        h2 = tok[:, :, 0:D]
        gate = sb("gate", [P, 2, D])
        wring = sb("wring", [P, WSLOTS, KD, CH])
        skr = sb("skr", [P, 512])
        diag = sb("diag", [P, GR * GU, P])
        modT = sb("modT", [P, 48, 2])
        mrow = skr[0:2, :]
        scl = sb("scl", [P, 2, KD, 2])
        xo = sb("xo", [P, 2, D])
        ocat, oT = xo[:, 0, :], xo[:, 1, :]
        sq = sb("sq", [P, 512])
        small = sb("small", [P, 520])

        dn_tok = sb("dn_tok", [P, NT, 1536])
        z = sb("z", [P, NT, 512])
        ops = sb("ops", [P, 4096])
        qTa = ops[:, 0:1536].rearrange("p (h n) -> p h n", h=DA_H)
        vca = ops[:, 1536:2048]
        kTa = ops[:, 2048:4096].rearrange("p (h n) -> p h n", h=DA_H)
        E = sb("E", [P, 2, 2, 3 * P])
        aT = sb("aT", [P, 3 * P])

        big = sb("big", [P, GR * GU * 2 * D])
        rows = big[:, :].rearrange("p (s w) -> p s w", w=2 * D)
        pre = big[:, 0:1170].rearrange("p (s n) -> p s n", s=3)
        cy = big[:, 1176:2334].rearrange("p (s n) -> p s n", s=3)
        cz = big[:, 2336:3494].rearrange("p (s n) -> p s n", s=3)
        cjunk = big[:, 3584:3712]
        wb = big[:, 3712:3840].rearrange("p (k c) -> p k c", k=KD)

        def heads(ap):
            return ap.rearrange("p (h n) -> p h n", h=4)

        wflat = wring[:, :, :, :].rearrange("p s k c -> p (s k c)")
        EG, DT, LT, TM, TT, PM, VB, KBG = [
            [[home[:, (d * 8 + i) * 512:(d * 8 + i + 1) * 512] for d in range(2)] for home in (big, big, wflat)]
            for i in range(8)]
        KDK = LT
        dqT = big[:, 8192:9728].rearrange("p (t c) -> p t c", t=NT)
        dkT = big[:, 9728:11264].rearrange("p (t c) -> p t c", t=NT)
        S = dn_tok[:, 0, 512:1536].rearrange("p (d c) -> p d c", d=2)

        def qk(pi, t):
            return (dqT[:, t, :], dkT[:, t, :]) if pi < 2 else (tok[:, t, 0:512], tok[:, t, 512:1024])


        spare = hT[:, 1:3].rearrange("p t k n -> p (t k n)")

        def sco(t, hh):
            return (xo[:, hh, :], ops[:, 2048 + 1024 * hh:3072 + 1024 * hh],
                    ops[:, 1024 * hh:1024 * hh + 1024])[t]

        def pqT(t, n):
            return spare[:, 1424:1936] if t == 0 else dn_tok[:, 1, 512 + 512 * (n % 2):1024 + 512 * (n % 2)]

        firsts = [spare[:, 0:512], dn_tok[:, 0, 0:512], dn_tok[:, 2, 512:1024]]
        seconds = [spare[:, 512:1424]] + [dn_tok[:, 0, 512:1424]] * 2
        sv = [f[:, 0:256] for f in firsts]
        siu = [f[:, 256:512].bitcast(u32) for f in firsts]
        e01 = [f[:, 256:512] for f in firsts]
        sif = [f[:, 0:256] for f in seconds]
        phf = [f[:, 256:512] for f in seconds]
        phl = [f[:, 256:512].bitcast(u32) for f in seconds]
        sv2 = [f[:, 512:640] for f in seconds]
        gex = [f[:, 640:768] for f in seconds]
        pos = [f[:, 768:896].bitcast(u32) for f in seconds]
        gsm = [f[:, 896:912] for f in seconds]

        idx = [sb("idx", [P, SLOTS], i32)] + [K[:, C_NBF + P * i:C_NBF + P * (i + 1)].bitcast(i32) for i in range(2)]
        gates = [Q[:, Q_LAM + P * i:Q_LAM + P * (i + 1)] for i in range(2)] + [sb("gates", [P, SLOTS])]
        cur = sb("cur", [P, GR, GU], i32)
        dots = sb("dots", [P, GR, GU])
        gel = sb("gel", [P, GR, GU])

        used = [0]

        def sm(n):
            used[0] += n
            assert used[0] <= 520
            return small[:, used[0] - n:used[0]]

        def by_tile(ap):
            return ap.rearrange("p (t c) -> p t c", t=NT)

        cs, ssq, rst = sm(16), sm(6), sm(6)
        ssk, rnk = sm(24), sm(24)
        ba = by_tile(sm(48))
        beta, gg, g1, g2, gc, eg, bg = [by_tile(sm(24)) for _ in range(7)]
        nea, last, kds, kde = sm(8), sm(8), sm(8), sm(8)
        mx, nmx, zz, rz = sm(8), sm(8), sm(8), sm(8)
        lamv, lam = sm(4), sm(2)
        ob, obr = sm(4), sm(4)
        sub08 = Q[:, Q_SUB:Q_SUB + P]
        fss, fr = sm(1), sm(1)

        bank = [ctx.enter_context(nc.psum_tensor(f"bank{i}", [P, 512], f32)) for i in range(8)]
        acc = bank[0:2]

        def ps(*job):
            return bank[RING0 + counts.jobs.get(job, 0) % RINGN]

        chunk_in = [sem(f"chunk_in{i}") for i in range(WSLOTS)]
        params_in, consts_in, x_in, kv_in, s0_in, nout_in = [
            sem(n) for n in ("params_in", "consts_in", "x_in", "kv_in", "s0_in", "nout_in")]
        cache_out, state_out, y_out = sem("cache_out"), sem("state_out"), sem("y_out")
        product = signal("product")
        sk_in = sem("sk_in")
        c_silu, squares, rstd_in, rstd_out, xn_ready, hT_ready, mrow_ready, modulated, mod_ready, scl_ready, gateb, gate_ready = [
            signal(n) for n in ("c_silu", "squares", "rstd_in", "rstd_out", "xn_ready", "hT_ready", "mrow_ready", "modulated", "mod_ready",
                                "scl_ready", "gateb", "gate_ready")]
        pads, pre_ready, conv_ready, silu_ready, ctok_ready, knorm_in, knorm_out, kscaled = [
            signal(n) for n in ("pads", "pre_ready", "conv_ready", "silu_ready", "ctok_ready", "knorm_in",
                                "knorm_out", "kscaled")]
        ba_ready, beta_ready, softplus_in, softplus_out, g_ready, gc_ready, eg_ready, bg_ready = [
            signal(n) for n in ("ba_ready", "beta_ready", "softplus_in", "softplus_out", "g_ready", "gc_ready",
                                "eg_ready", "bg_ready")]
        qkT_ready, tok_ready, roped, daT_ready, kept = [
            signal(n) for n in ("qkT_ready", "tok_ready", "roped", "daT_ready", "kept")]
        bc_ready, egrow_ready, kde_ready, dd_ready, dt_ready, kds_ready, lt_ready, at_ready = [
            signal(n) for n in ("bc_ready", "egrow_ready", "kde_ready", "dd_ready", "dt_ready", "kds_ready",
                                "lt_ready", "at_ready")]
        dn_pool, p_ready, t_ready, nw_ready, vn_ready, osum_ready, s_ready = [
            signal(n) for n in ("dn_pool", "p_ready", "t_ready", "nw_ready", "vn_ready", "osum_ready", "s_ready")]
        lam_in, lam_exp, mx_ready, e_ready, a_ready, aT_ready, av_ready = [
            signal(n) for n in ("lam_in", "lam_exp", "mx_ready", "e_ready", "a_ready", "aT_ready", "av_ready")]
        on_in, on_out, ocat_ready, oT_ready, x2_ready, h2_ready = [
            signal(n) for n in ("on_in", "on_out", "ocat_ready", "oT_ready", "x2_ready", "h2_ready")]
        pq_ready, sco_ready, gx_in, gx_out, idx_ready = [
            signal(n) for n in ("pq_ready", "sco_ready", "gx_in", "gx_out", "idx_ready")]
        rows_in = [sem(f"rows_in{r}") for r in range(GR)]
        gather_go = sem("gather_go")
        cur_ready, dot_ready, gelu_ready, diag_ready, vsum_done = [
            sem(n) for n in ("cur_ready", "dot_ready", "gelu_ready", "diag_ready", "vsum_done")]
        acc_done, acc_read, y_ready, fin_in, fin_out = [
            signal(n) for n in ("acc_done", "acc_read", "y_ready", "fin_in", "fin_out")]
        dve_step, act_step, pool_step = sem("dve_step"), sem("act_step"), sem("pool_step")

        def linker(eng, step):
            n = [0]

            def link(ins):
                n[0] += 1
                ins.then_inc(step, 1)
                eng.wait_ge(step, n[0])
            return link

        def reads(sig, key, *job):
            counts.release[job] = (sig.name, key)
            return sig.next(*key)

        def chunk(*name):
            return wring[:, CHUNK_NO[name] % WSLOTS]

        def chunk_here(*name):
            n = CHUNK_NO[name]
            return chunk_in[n % WSLOTS], 16 * (n // WSLOTS + 1)

        def col(ap, n):
            return ap.unsqueeze(2).to_broadcast([P, ap.shape[1], n])

        def rep(ap, n):
            return ap.unsqueeze(1).to_broadcast([P, n, ap.shape[1]])

        block = ctx.enter_context(nc.Block())
        STEPS = schedule()
        last_use = {("mod", m, 0): ("mod", m) for m in range(12)}
        last_use.update({("dn", i, 0): ("chT", 4 * i + 3) for i in range(3)})
        last_use.update({("z", 0, 0): ("tok", 3, 2)})
        last_use.update({("da", c, 0): ("tok", c, 2) for c in range(3)})
        last_use.update({("out", h, ps): ("wo", 2 * ps, h) for h in range(2) for ps in range(2)})
        last_use.update({("pq", i, ps): ("pq", i, 2 * ps) for i in range(4) for ps in range(2)})

        def run(parts):
            for step in STEPS:
                if step[0] in parts:
                    parts[step[0]](*step[1:])

        @block.sync
        def _(sp):
            sp.dma_start(Q[:, :], par).then_inc(params_in, 16)
            sp.dma_start(xs[:, :, :], x).then_inc(x_in, 16)
            sp.dma_start(K[:, :], cst).then_inc(consts_in, 16)
            sp.dma_start(wb[:, :, :], wba).then_inc(consts_in, 16)
            for n, name in enumerate(CHUNKS):
                if n >= WSLOTS:
                    sp.wait_ge(*product.at(*last_use[CHUNKS[n - WSLOTS]]))
                if name == ("out", 0, 1):
                    sp.wait_ge(*product.at("o", *PAIRS[2][1]))
                src = STORED.index(name[:2] + (0,))
                sp.dma_start(wring[:, n % WSLOTS], wch[src]).then_inc(chunk_in[n % WSLOTS], 16)
                if n == 8:
                    sp.dma_start(kTa[:, :, P:2 * P], kcT).then_inc(kv_in, 16)
                    sp.dma_start(vca, vc).then_inc(kv_in, 16)
                    sp.dma_start(M[:, :], msk).then_inc(kv_in, 16)
                if name[0] == "pq":
                    _, i, again = name
                    if i == 0 and not again:
                        sp.wait_ge(*product.at("modT", 11))
                    else:
                        sp.wait_ge(*product.at("s", (i - 1) % 4, 2 * again if i else 0))
                    sp.dma_start(skr[:, :], subk[i]).then_inc(sk_in, 16)
            sp.wait_ge(*squares.at(1, 2))
            sp.wait_ge(*product.at("xT", 1, 2, 1))
            sp.dma_start(xo[:, 1, :], nout).then_inc(nout_in, 16)
            for t in range(NT):
                sp.wait_ge(*y_ready.at(t))
                sp.dma_start(y[t], xs[:, t, :]).then_inc(y_out, 16)
            sp.wait_ge(y_out, 16 * NT)
            sp.wait_ge(cache_out, 32)
            sp.wait_ge(state_out, 32)

        @block.gpsimd
        def _(pool):
            link = linker(pool, pool_step)
            nc.gpsimd.memset(pre[:, :, :], 0.0).then_inc(*pads.next())

            def token(c, t):
                if (c, t) == (2, 0):
                    pool.wait_ge(*tok_ready.at(2, 0))
                    pool.dma_start(o_ck, tok[:, 0, 512:1024]).then_inc(cache_out, 16)
                    pool.dma_start(o_cv, tok[:, 0, 1024:1536]).then_inc(cache_out, 16)

            def rope(t):
                if t == 1:
                    pool.wait_ge(consts_in, 32)
                    pool.wait_ge(*product.at("xT", 0, 2, 1))
                pool.wait_ge(*tok_ready.at(1, t))
                rt = xo[:, :, :].rearrange("p a (b n) -> p (a b) n", b=2)

                def table(c):
                    v = K[:, c + (t - 1) * 32:c + t * 32].rearrange("p (a f) -> p a f", a=2)
                    return v.unsqueeze(1).to_broadcast([P, 16, 2, 16])

                def half(i):
                    v = tok[:, t, 0:1024].rearrange("p (h a i f) -> p h a i f", h=16, a=2, i=2)
                    return v[:, :, :, i, :]

                tv = [rt[:, i, :].rearrange("p (h a f) -> p h a f", h=16, a=2) for i in range(4)]
                nc.gpsimd.tensor_tensor(tv[0], half(0), table(C_COS), ALU.mult)
                nc.gpsimd.tensor_tensor(tv[1], half(1), table(C_SIN), ALU.mult)
                nc.gpsimd.tensor_tensor(tv[2], half(1), table(C_COS), ALU.mult)
                link(nc.gpsimd.tensor_tensor(tv[3], half(0), table(C_SIN), ALU.mult))
                nc.gpsimd.tensor_tensor(half(0), tv[0], tv[1], ALU.subtract)
                nc.gpsimd.tensor_tensor(half(1), tv[2], tv[3], ALU.add).then_inc(*roped.next(t))
                pool.wait_ge(*roped.at(t))

            def keep_qk():
                pool.wait_ge(*product.at("daT", 2, 1))
                pool.wait_ge(*qkT_ready.at(2, 1))
                nc.gpsimd.tensor_copy(tok[:, 1:3, 0:512], dqT[:, 1:3, :])
                nc.gpsimd.tensor_copy(tok[:, 1:3, 512:1024], dkT[:, 1:3, :]).then_inc(*kept.next())

            def dn_scale(pi):
                for t, d in PAIRS[pi]:
                    k4, v4 = heads(dn_tok[:, t, 512:1024]), heads(dn_tok[:, t, 1024:1536])
                    c4 = slice(4 * d, 4 * d + 4)
                    if pi == 0:
                        pool.wait_ge(*kscaled.at(2))
                        pool.wait_ge(*ctok_ready.at(11))
                        pool.wait_ge(*bg_ready.at())
                    elif pi == 1:
                        pool.wait_ge(*vn_ready.at(*PAIRS[0][d]))
                    else:
                        pool.wait_ge(*product.at("pq", 3, 0))
                    nc.gpsimd.tensor_tensor(heads(VB[pi][d]), v4, col(beta[:, t, c4], P), ALU.mult
                                            ).then_inc(*dn_pool.next("vb", t, d))
                    nc.gpsimd.tensor_tensor(heads(KBG[pi][d]), k4, col(bg[:, t, c4], P), ALU.mult
                                            ).then_inc(*dn_pool.next("kbg", t, d))

            def dn_decay(pi):
                for t, d in PAIRS[pi]:
                    c4 = slice(4 * d, 4 * d + 4)
                    edge = P - 1 if d == 0 else 0
                    pool.wait_ge(*egrow_ready.at(t, d))
                    if pi == 2:
                        pool.wait_ge(*s_ready.at(*PAIRS[1][d]))
                    nc.gpsimd.tensor_copy(last[:, c4], heads(EG[pi][d])[:, :, edge]).then_inc(*dn_pool.next("last", t, d))
                    pool.wait_ge(*dn_pool.at("last", t, d))
                    pool.wait_ge(*qkT_ready.at(t, 0))
                    nc.gpsimd.tensor_tensor(EG[pi][d], EG[pi][d], qk(pi, t)[0], ALU.mult).then_inc(*dn_pool.next("qg", t, d))

            def dn_w(pi):
                for t, d in PAIRS[pi]:
                    if updates_state(t, d):
                        pool.wait_ge(*kds_ready.at(t, d))
                        pool.wait_ge(*product.at("P", t, d, LEVELS - 1))
                        nc.gpsimd.tensor_tensor(heads(KDK[pi][d]), heads(dn_tok[:, t, 512:1024]),
                                                col(kds[:, 4 * d:4 * d + 4], P), ALU.mult
                                                ).then_inc(*dn_pool.next("kd", t, d))

            def first_states():
                for d in range(2):
                    pool.wait_ge(*s_ready.at(0, d))
                    pool.dma_start((o_sf, o_sb)[d], S[:, d, :]).then_inc(state_out, 16)
                pool.wait_ge(state_out, 32)
                pool.dma_start(S[:, :, :], s0).then_inc(s0_in, 16)

            def gather(t, n, g, r, held):
                if held:
                    pool.wait_ge(vsum_done, g - (GR - 1))
                nc.gpsimd.tensor_copy(cur[:, r, :], idx[t][:, bass.ds(n * GU, GU)]).then_inc(cur_ready, 1)
                pool.wait_ge(cur_ready, g + 1)
                pool.sem_inc(gather_go, 1)
                for u in range(GU):
                    nc.gpsimd.indirect_dma_start(
                        rows[:, r * GU + u, :], None, uv,
                        bass.IndirectOffsetOnAxis(ap=cur[:, r, u:u + 1], axis=0)).then_inc(rows_in[r], 16)

            def peer(t, n):
                if (t, n) in ((0, 0), (0, SLOTS // 2), (1, 0)):
                    pool.wait_ge(*idx_ready.at(t, 0 if (t, n) == (0, 0) else 1))
                g = t * SLOTS + n
                gather(t, n, g, g % GR, g >= GR)

            run({"token": token, "rope": rope, "dn_scale": dn_scale, "dn_decay": dn_decay, "dn_w": dn_w, "keep_qk": keep_qk,
                 "first_states": first_states, "peer": peer})
            for t, first in ((1, MIXED), (2, 0)):
                g0 = t * SLOTS + first
                if t == 2:
                    pool.wait_ge(*idx_ready.at(2, 1))
                rounds, rest = in_rounds(first, SLOTS)
                with pool.Fori(0, rounds) as i:
                    for r in range(GR):
                        gather(t, i * GR + (first + r), i * GR + (g0 + r), (g0 + r) % GR, True)
                for n in rest:
                    gather(t, n, t * SLOTS + n, (t * SLOTS + n) % GR, True)

        @block.scalar
        def _(act):
            link = linker(act, act_step)

            def evac(out, job, sig, key, func=ACT.Copy, n=512, src=None, **kw):
                act.wait_ge(*product.at(*job))
                nc.scalar.activation(out, ps(*job)[:, 0:n] if src is None else src, func, **kw
                                     ).then_inc(*reads(sig, key, *job))

            act.wait_ge(params_in, 16)
            nc.scalar.activation(cs, Q[:, Q_C:Q_C + 16], ACT.Silu).then_inc(*c_silu.next())
            act.wait_ge(x_in, 16)

            def norm(w, t):
                if w:
                    act.wait_ge(*x2_ready.at(t, 1))
                c = slice(3 * w + t, 3 * w + t + 1)
                nc.scalar.activation(xo[:, 1, :], xs[:, t, :], ACT.Square, accum_out=ssq[:, c]
                                     ).then_inc(*squares.next(w, t))
                act.wait_ge(*rstd_in.at(w, t))
                nc.scalar.activation(rst[:, c], ssq[:, c], ACT.Sqrt).then_inc(*rstd_out.next(w, t))

            def mod(m):
                job = ("mod", m)
                act.wait_ge(*product.at(*job))
                if m:
                    act.wait_ge(*product.at("modT", m - 1))
                nc.scalar.activation(mrow[:, :], ps(*job)[0:2, :], ACT.Copy).then_inc(*reads(mrow_ready, (m,), *job))

            def x_copy(w, t):
                if w:
                    act.wait_ge(*scl_ready.at(1))
                for h in range(2):
                    job = ("xT", w, t, h)
                    if w == 0:
                        evac(hT[:, t, 4 * h:4 * h + 4, :], job, hT_ready, (0, t, h), src=heads(ps(*job)[:, :]))
                    else:
                        act.wait_ge(*product.at(*job))
                        by_feature(t, 1, range(4 * h, 4 * h + 4), heads(ps(*job)[:, :])
                                   ).then_inc(*reads(hT_ready, (1, t, h), *job))

            def by_feature(t, w, ks, src):
                v = min(t, 1)
                for i, k in enumerate(ks):
                    ins = nc.scalar.activation(hT[:, t, k, :], src[:, i, :], ACT.Identity,
                                               bias=modT[:, 24 * w + k, v:v + 1], scale=scl[:, w, k, v:v + 1])
                return ins

            def modulate():
                act.wait_ge(*scl_ready.at(0))
                act.wait_ge(*hT_ready.at(0, 0, 1))
                by_feature(0, 0, range(KD), hT[:, 0]).then_inc(*modulated.next(0))

            def channels(b):
                job = ("chT", b)
                act.wait_ge(*product.at(*job))
                if b == 0:
                    act.wait_ge(*pads.at())
                if b >= 3:
                    act.wait_ge(*conv_ready.at(b - 3))
                nc.scalar.activation(pre[:, b % 3, 2:130], ps(*job)[:, 0:P], ACT.Copy)
                nc.scalar.activation(pre[:, b % 3, 132:388], ps(*job)[:, P:T], ACT.Copy
                                     ).then_inc(*reads(pre_ready, (b,), *job))

            def silu(b):
                act.wait_ge(*conv_ready.at(b))
                if b >= 3:
                    act.wait_ge(*product.at("cT", b - 3))
                nc.scalar.activation(cz[:, b % 3, :], cy[:, b % 3, :], ACT.Silu).then_inc(*silu_ready.next(b))

            def c_turn(c):
                job = ("cT", c)
                act.wait_ge(*product.at(*job))
                v = ps(*job)[:, 0:T].rearrange("p (t n) -> p t n", t=NT)
                if c < 8:
                    for t in range(NT):
                        link(nc.scalar.activation(cjunk, v[:, t, :], ACT.Square,
                                                  accum_out=ssk[:, 8 * t + c:8 * t + c + 1]))
                nc.scalar.activation(dn_tok[:, :, c * P:(c + 1) * P], v, ACT.Copy
                                     ).then_inc(*reads(ctok_ready, (c,), *job))

            def gate_in():
                for t in range(NT):
                    evac(ba[:, t, :], ("ba", t), ba_ready, (t,), n=16)
                act.wait_ge(*ba_ready.at(2))
                nc.scalar.activation(beta[:, :, :], ba[:, :, 0:8], ACT.Sigmoid).then_inc(*beta_ready.next())
                act.wait_ge(*knorm_in.at())
                nc.scalar.activation(rnk, ssk, ACT.Sqrt).then_inc(*knorm_out.next())
                act.wait_ge(*softplus_in.at())
                link(nc.scalar.activation(g1[:, :, :], g1[:, :, :], ACT.Exp))
                link(nc.scalar.activation(g1[:, :, :], g1[:, :, :], ACT.Ln, bias=1.0))
                nc.scalar.activation(nea, Q[:, Q_ALOG:Q_ALOG + 8], ACT.Exp).then_inc(*softplus_out.next())

            def decay():
                for t in range(NT):
                    evac(gc[:, t, :], ("gc", t), gc_ready, (t,), n=8)
                act.wait_ge(*gc_ready.at(2))
                nc.scalar.activation(eg[:, :, :], gc[:, :, :], ACT.Exp).then_inc(*eg_ready.next())

            def qk_turn(t):
                for w in range(2):
                    evac((dqT, dkT)[w][:, t, :], ("qkT", t, w), qkT_ready, (t, w))

            def token(c, t):
                if c == 3:
                    evac(z[:, t, :], ("tok", c, t), tok_ready, (c, t), func=ACT.Silu)
                else:
                    evac(tok[:, t, c * 512:(c + 1) * 512], ("tok", c, t), tok_ready, (c, t))

            def da_turn(t):
                if t == 0:
                    act.wait_ge(kv_in, 48)
                for w in range(2):
                    o = t * P if w == 0 else (0, 2 * P, 3 * P)[t]
                    job = ("daT", t, w)
                    evac((qTa, kTa)[w][:, :, o:o + P], job, daT_ready, (t, w), src=heads(ps(*job)[:, :]))

            def gate_rows(w, v, h):
                if w:
                    act.wait_ge(*x2_ready.at(2 * v, 1))
                evac(gate[:, v, h * 512:(h + 1) * 512], ("gate", w, v, h), gate_ready, (w, v, h))

            def lam_step():
                act.wait_ge(*lam_in.at())
                nc.scalar.activation(lamv[:, 2:4], lamv[:, 0:2], ACT.Exp).then_inc(*lam_exp.next())

            def dn_decay(pi):
                for t, d in PAIRS[pi]:
                    job = ("gr", t, d)
                    act.wait_ge(*product.at(*job))
                    if pi == 1:
                        act.wait_ge(*product.at("o", *PAIRS[0][d]))
                    elif pi:
                        act.wait_ge(*product.at("pq", 3, 0))
                    else:
                        act.wait_ge(*product.at("cT", 11))
                        act.wait_ge(*ctok_ready.at(11))
                    nc.scalar.activation(EG[pi][d], ps(*job)[:, :], ACT.Exp).then_inc(*egrow_ready.next(t, d))
                for t, d in PAIRS[pi]:
                    c4 = slice(4 * d, 4 * d + 4)
                    act.wait_ge(*kde_ready.at(t, d))
                    if pi:
                        act.wait_ge(*dn_pool.at("kd", *PAIRS[pi - 1][d]))
                    nc.scalar.activation(kds[:, c4], kde[:, c4], ACT.Exp).then_inc(*kds_ready.next(t, d))
                    act.wait_ge(*dd_ready.at(t, d))
                    nc.scalar.activation(DT[pi][d], DT[pi][d], ACT.Exp).then_inc(*dt_ready.next(t, d))

            def dn_w(pi):
                for t, d in PAIRS[pi]:
                    if has_state(t, d):
                        evac(PM[pi][d], ("wT", t, d), nw_ready, (t, d), scale=-1.0)

            def expo(t, h):
                nk = P if t == 0 else 3 * P
                n = t * DA_H + h
                act.wait_ge(*mx_ready.at(t, h))
                if n >= 2:
                    act.wait_ge(*product.at("aT", *divmod(n - 2, DA_H)))
                if h == 0 and t:
                    act.wait_ge(*a_ready.at(t - 1, 3))
                for m in range(2):
                    c = slice(2 * h + m, 2 * h + m + 1)
                    job = ("sc", t, 2 * h + m)
                    nc.scalar.activation(E[:, h % 2, m, 0:nk], ps(*job)[:, 0:nk], ACT.Exp,
                                         bias=nmx[:, c], scale=DA_DH ** -0.5, accum_out=zz[:, c]
                                         ).then_inc(*reads(e_ready, (t, 2 * h + m), *job))

            def a_copy(t, h):
                nk = P if t == 0 else 3 * P
                n = t * DA_H + h
                if n:
                    act.wait_ge(*product.at("av", *divmod(n - 1, DA_H)))
                evac(aT[:, 0:nk], ("aT", t, h), aT_ready, (t, h), n=nk)

            def head_norm(t, g):
                act.wait_ge(*on_in.at(t, g))
                nc.scalar.activation(obr, ob, ACT.Sqrt).then_inc(*on_out.next(t, g))

            def o_copy(t):
                for h in range(2):
                    evac(oT[:, h * 512:(h + 1) * 512], ("oT", t, h), oT_ready, (t, h))

            def h_copy(t):
                if t == 0:
                    act.wait_ge(cache_out, 32)
                for h in range(2):
                    evac(h2[:, t, h * 512:(h + 1) * 512], ("h2", t, h), h2_ready, (t, h))

            unit = [0]

            def q_copy(i, t):
                n = unit[0]
                unit[0] += 1
                before = retrieval_units.index((i, t)) - (1 if t == 0 else 2)
                if before >= 0:
                    act.wait_ge(*product.at("s", *retrieval_units[before]))
                evac(pqT(t, i * 2 + t), ("pq", i, t), pq_ready, (i, t))

            def s_copy(i, t):
                hh = i // 2
                o = 512 * (i % 2)
                evac(sco(t, hh)[:, o:o + 512], ("s", i, t), sco_ready, (i, t))

            def exponentials(t, hh):
                act.wait_ge(*gx_in.at(t, hh))
                g = gex[t][:, 64 * hh:64 * hh + 64]
                nc.scalar.activation(g, g, ACT.Exp).then_inc(*gx_out.next(t, hh))

            def gelu(g, r):
                act.wait_ge(dot_ready, g + 1)
                nc.scalar.activation(gel[:, r, :], dots[:, r, :], ACT.Gelu).then_inc(gelu_ready, 1)

            def last_root(t):
                act.wait_ge(*fin_in.at(t))
                nc.scalar.activation(fr, fss, ACT.Sqrt).then_inc(*fin_out.next(t))

            retrieval_units = [(i, 0) for i in range(4)] + [(i, t) for i in range(4) for t in (1, 2)]
            run({"norm": norm, "mod": mod, "modulate": modulate, "x_copy": x_copy, "channels": channels, "silu": silu, "c_turn": c_turn,
                 "gate_in": gate_in, "decay": decay, "qk_turn": qk_turn, "token": token, "da_turn": da_turn,
                 "gate": gate_rows, "lam": lam_step, "dn_decay": dn_decay, "dn_w": dn_w, "expo": expo,
                 "a_copy": a_copy, "head_norm": head_norm, "o_copy": o_copy, "h_copy": h_copy, "q_copy": q_copy,
                 "s_copy": s_copy, "places": exponentials, "peer": lambda t, n: gelu(t * SLOTS + n, (t * SLOTS + n) % GR),
                 "last_norm": last_root})

            for t, first in ((1, MIXED), (2, 0)):
                g0 = t * SLOTS + first
                rounds, rest = in_rounds(first, SLOTS)
                with act.Fori(0, rounds) as i:
                    for r in range(GR):
                        gelu(i * GR + (g0 + r), (g0 + r) % GR)
                for n in rest:
                    gelu(t * SLOTS + n, (t * SLOTS + n) % GR)
                last_root(t)

        @block.tensor
        def _(pe):
            order = []

            def begin(*job):
                n = len(order)
                counts.jobs[job] = n
                if n >= RINGN:
                    got = counts.release.get(order[n - RINGN])
                    if got:
                        pe.wait_ge(*signals[got[0]].at(*got[1]))
                order.append(job)
                return bank[RING0 + n % RINGN]

            def end(ins, *job):
                ins.then_inc(*product.next(*job))

            def mm(out, lhsT, rhs, first=True, last=True):
                return nc.tensor.matmul(out, lhsT, rhs, start=first, stop=last)

            def turn(src, *job, n=4):
                b = begin(*job)
                for i in range(n):
                    ins = nc.tensor.transpose(b[:, i * P:(i + 1) * P], src[:, i * P:(i + 1) * P], ident)
                end(ins, *job)

            def mod(m):
                if m == 0:
                    pe.wait_ge(*c_silu.at())
                pe.wait_ge(*chunk_here("mod", m, 0))
                b = begin("mod", m)
                for k in range(KD):
                    ins = mm(b[0:2, :], cs[:, 2 * k:2 * k + 2], chunk("mod", m, 0)[:, k, :], k == 0, k == KD - 1)
                end(ins, "mod", m)

            def mod_turn(m):
                pe.wait_ge(*mrow_ready.at(m))
                b = begin("modT", m)
                for i in range(4):
                    ins = nc.tensor.transpose(b[:, 2 * i:2 * i + 2], mrow[:, i * P:(i + 1) * P], ident[0:2, 0:2])
                end(ins, "modT", m)

            def x_turn(w, t):
                if (w, t) == (0, 0):
                    pe.wait_ge(consts_in, 32)
                pe.wait_ge(*xn_ready.at(w, t))
                for h in range(2):
                    turn(xo[:, 0, h * 512:(h + 1) * 512], "xT", w, t, h)

            def channels(c):
                if c == 0:
                    for t in range(NT):
                        pe.wait_ge(*modulated.at(t))
                pe.wait_ge(*chunk_here("dn", c // 4, 0))
                b = begin("chT", c)
                w = chunk("dn", c // 4, 0)
                o = (c % 4) * P
                for k in range(KD):
                    ins = mm(b[:, 0:T].rearrange("p (t n) -> p t n", t=NT), w[:, k, o:o + P], hT[:, :, k, :],
                             k == 0, k == KD - 1)
                end(ins, "chT", c)

            def c_turn(c):
                pe.wait_ge(*silu_ready.at(c))
                b = begin("cT", c)
                for t in range(NT):
                    o = (0, 130, 258)[t]
                    ins = nc.tensor.transpose(b[:, t * P:(t + 1) * P], cz[:, c % 3, o:o + P], ident)
                end(ins, "cT", c)

            def gate_in():
                for t in range(NT):
                    b = begin("ba", t)
                    for k in range(KD):
                        ins = mm(b[:, 0:16], hT[:, t, k, :], wb[:, k, :], k == 0, k == KD - 1)
                    end(ins, "ba", t)

            def decay():
                pe.wait_ge(*g_ready.at())
                for t in range(NT):
                    b = begin("gc", t)
                    for d in range(2):
                        ins = mm(b[:, 4 * d:4 * d + 4], tri[d], gg[:, t, 4 * d:4 * d + 4])
                    end(ins, "gc", t)

            def qk_turn(t):
                pe.wait_ge(*kscaled.at(t))
                for w in range(2):
                    turn(dn_tok[:, t, w * 512:(w + 1) * 512], "qkT", t, w)

            def token(c, t):
                kind = ("da", c, 0) if c < 3 else ("z", 0, 0)
                pe.wait_ge(*chunk_here(*kind))
                b = begin("tok", c, t)
                for k in range(KD):
                    ins = mm(b[:, :], hT[:, t, k, :], chunk(*kind)[:, k, :], k == 0, k == KD - 1)
                end(ins, "tok", c, t)

            def da_turn(t):
                pe.wait_ge(*(roped.at(t) if t else tok_ready.at(1, 0)))
                for w in range(2):
                    turn(tok[:, t, w * 512:(w + 1) * 512], "daT", t, w)

            def gate_rows(w, v, h):
                pe.wait_ge(*gateb.at(w, v, h))
                turn(sq[:, :], "gate", w, v, h)

            def per_head(job, terms):
                b = begin(*job)
                for h in range(4):
                    s = slice(h * P, (h + 1) * P)
                    for i, (l, r) in enumerate(terms):
                        ins = mm(b[:, s], l[:, s], r[:, s], i == 0, i == len(terms) - 1)
                end(ins, *job)

            def dn_decay(pi):
                for t, d in PAIRS[pi]:
                    pe.wait_ge(*bc_ready.at("g", t, d))
                    b = begin("gr", t, d)
                    for h in range(4):
                        ins = mm(b[:, h * P:(h + 1) * P], LT[pi][d][:, h * P:(h + 1) * P], tri[d])
                    end(ins, "gr", t, d)

            def dn_scores(pi):
                for t, d in PAIRS[pi]:
                    pe.wait_ge(*(qkT_ready.at(t, 1) if pi < 2 else kept.at()))
                    per_head(("kk", t, d), [(qk(pi, t)[1], qk(pi, t)[1])])
                for t, d in PAIRS[pi]:
                    pe.wait_ge(*bc_ready.at("b", t, d))
                    turn(PM[pi][d], "br", t, d)
                for t, d in PAIRS[pi]:
                    per_head(("qk", t, d), [(qk(pi, t)[1], qk(pi, t)[0])])

            def dn_p(pi, lv):
                for t, d in PAIRS[pi]:
                    if lv == 0:
                        pe.wait_ge(*lt_ready.at(t, d))
                        turn(LT[pi][d], "P", t, d, 0)
                    else:
                        pe.wait_ge(*t_ready.at("T", t, d, lv - 1))
                        per_head(("P", t, d, lv), [(LT[pi][d], TM[pi][d])])

            def dn_t(pi, lv):
                for t, d in PAIRS[pi]:
                    pe.wait_ge(*p_ready.at(t, d, lv))
                    if lv == 0:
                        turn(PM[pi][d], "TT", t, d, 0)
                    else:
                        pe.wait_ge(*t_ready.at("TT", t, d, lv - 1))
                        if lv < LEVELS - 1:
                            per_head(("T", t, d, lv), [(TT[pi][d], PM[pi][d])])
                        per_head(("TT", t, d, lv), [(PM[pi][d], TT[pi][d])])

            def dn_w(pi):
                for t, d in PAIRS[pi]:
                    if has_state(t, d):
                        pe.wait_ge(*t_ready.at("TT", t, d, LEVELS - 1))
                        pe.wait_ge(*dn_pool.at("kbg", t, d))
                        per_head(("wT", t, d), [(KBG[pi][d], TT[pi][d])])

            def dn_v(pi):
                for t, d in PAIRS[pi]:
                    pe.wait_ge(*t_ready.at("TT", t, d, LEVELS - 1))
                    pe.wait_ge(*dn_pool.at("vb", t, d))
                    if has_state(t, d):
                        pe.wait_ge(*nw_ready.at(t, d))
                        pe.wait_ge(s0_in, 16)
                        if pi == 2:
                            pe.wait_ge(*s_ready.at(*PAIRS[1][d]))
                        per_head(("vn", t, d), [(TT[pi][d], VB[pi][d]), (PM[pi][d], S[:, d, :])])
                    else:
                        per_head(("vn", t, d), [(TT[pi][d], VB[pi][d])])

            def dn_o(pi):
                for t, d in PAIRS[pi]:
                    pe.wait_ge(*at_ready.at(t, d))
                    pe.wait_ge(*vn_ready.at(t, d))
                    pe.wait_ge(*dn_pool.at("qg", t, d))
                    terms = [(EG[pi][d], S[:, d, :])] if has_state(t, d) else []
                    per_head(("o", t, d), terms + [(DT[pi][d], TM[pi][d])])

            def dn_s(pi):
                for t, d in PAIRS[pi]:
                    if updates_state(t, d):
                        pe.wait_ge(*dn_pool.at("kd", t, d))
                        per_head(("S", t, d), [(KDK[pi][d], TM[pi][d])])

            def score(t, h):
                nk, ko = (P, 0) if t == 0 else (3 * P, P)
                if t == 0 and h == 0:
                    pe.wait_ge(kv_in, 48)
                    pe.wait_ge(*daT_ready.at(2, 1))
                for m in range(2):
                    b = begin("sc", t, 2 * h + m)
                    s = slice(64 * m, 64 * m + 64)
                    ins = mm(b[:, 0:nk], qTa[s, h, t * P:(t + 1) * P], kTa[s, h, ko:ko + nk])
                    end(ins, "sc", t, 2 * h + m)

            def a_turn(t, h):
                pe.wait_ge(*a_ready.at(t, h))
                turn(E[:, h % 2, 0, :], "aT", t, h, n=1 if t == 0 else 3)

            def value(t, h):
                pe.wait_ge(*aT_ready.at(t, h))
                b = begin("av", t, h)
                s = slice(h * P, (h + 1) * P)
                s1 = slice(1024 + h * P, 1024 + (h + 1) * P)
                vals = [tok[:, 0, s1]] if t == 0 else [vca[:, s], tok[:, 1, s1], tok[:, 2, s1]]
                for j, v in enumerate(vals):
                    ins = mm(b[:, 0:P], aT[:, j * P:(j + 1) * P], v, j == 0, j == len(vals) - 1)
                end(ins, "av", t, h)

            def o_turn(t):
                pe.wait_ge(*ocat_ready.at(t, 1))
                for h in range(2):
                    turn(ocat[:, h * 512:(h + 1) * 512], "oT", t, h)

            def w_out(t, h):
                pe.wait_ge(*oT_ready.at(t, 1))
                name = ("out", h, min(t, 1))
                pe.wait_ge(*chunk_here(*name))
                b = begin("wo", t, h)
                for k in range(KD // 2):
                    mm(b[:, :], oT[:, k * P:(k + 1) * P], chunk(*name)[:, k, :], k == 0, False)

            def w_out_rest(t, h):
                b = ps("wo", t, h)
                for k in range(KD // 2, KD):
                    ins = mm(b[:, :], oT[:, k * P:(k + 1) * P], chunk("out", h, min(t, 1))[:, k, :], False, k == KD - 1)
                end(ins, "wo", t, h)

            def h_turn(t):
                pe.wait_ge(*hT_ready.at(1, t, 1))
                for h in range(2):
                    turn(hT[:, t, 4 * h:4 * h + 4, :].rearrange("p k n -> p (k n)"), "h2", t, h)

            def query(i, t):
                name = ("pq", i, min(t, 1))
                pe.wait_ge(*chunk_here(*name))
                w = chunk(*name)
                b = begin("pq", i, t)
                for j in range(2):
                    for k in range(KD):
                        mm(b[:, j * P:(j + 1) * P], w[:, k, j * P:(j + 1) * P], hT[:, t, k, :], k == 0, k == KD - 1)

            def query_rest(i, t):
                w, b = chunk("pq", i, min(t, 1)), ps("pq", i, t)
                for j in range(2, 4):
                    for k in range(KD):
                        ins = mm(b[:, j * P:(j + 1) * P], w[:, k, j * P:(j + 1) * P], hT[:, t, k, :],
                                 k == 0, k == KD - 1)
                end(ins, "pq", i, t)

            def key_score(i, t):
                pe.wait_ge(sk_in, 16 * (4 * min(t, 1) + i + 1))
                pe.wait_ge(*pq_ready.at(i, t))
                q = pqT(t, i * 2 + t)
                b = begin("s", i, t)
                for j in range(4):
                    ins = mm(b[:, j * P:(j + 1) * P], q[:, j * P:(j + 1) * P], skr[:, j * P:(j + 1) * P])
                end(ins, "s", i, t)

            def v_sum(g, r, first=False, last=False):
                pe.wait_ge(diag_ready, g + 1)
                for u in range(GU):
                    for h in range(2):
                        ins = mm(acc[h][:, :], diag[:, r * GU + u, :],
                                 rows[:, r * GU + u, D + h * 512:D + (h + 1) * 512],
                                 first and u == 0, last and u == GU - 1)
                ins.then_inc(vsum_done, 1)

            def follow(t, n):
                if n == 0 and t:
                    pe.wait_ge(*acc_read.at(t - 1))
                g = t * SLOTS + n
                v_sum(g, g % GR, n == 0, n == SLOTS - 1)

            def peer(t, n):
                if n >= LAG:
                    follow(t, n - LAG)

            def peer_end(t):
                for n in range(SLOTS - LAG, SLOTS):
                    follow(t, n)

            run({"mod": mod, "mod_turn": mod_turn, "x_turn": x_turn, "channels": channels, "c_turn": c_turn, "gate_in": gate_in,
                 "decay": decay, "qk_turn": qk_turn, "token": token, "da_turn": da_turn, "gate": gate_rows,
                 "dn_decay": dn_decay, "dn_scores": dn_scores, "dn_p": dn_p, "dn_t": dn_t, "dn_w": dn_w,
                 "dn_v": dn_v, "dn_o": dn_o, "dn_s": dn_s, "score": score, "a_turn": a_turn, "value": value,
                 "o_turn": o_turn, "w_out": w_out, "h_turn": h_turn, "query": query, "query_rest": query_rest, "w_out_rest": w_out_rest, "key_score": key_score,
                 "peer": peer, "peer_end": peer_end})
            for t, first in ((1, MIXED - LAG), (2, 1)):
                if t == 2:
                    follow(2, 0)
                g0 = t * SLOTS + first
                rounds, rest = in_rounds(first, SLOTS - 1)
                with pe.Fori(0, rounds) as i:
                    for r in range(GR):
                        v_sum(i * GR + (g0 + r), (g0 + r) % GR)
                for n in [*rest, SLOTS - 1]:
                    follow(t, n)

        @block.vector
        def _(dve):
            link = linker(dve, dve_step)
            V = nc.vector
            H = PEER_H // 2
            sq_reader = []

            def sq_free():
                if sq_reader:
                    dve.wait_ge(*product.at(*sq_reader.pop()))

            def norm(w, t):
                c = slice(3 * w + t, 3 * w + t + 1)
                dve.wait_ge(*squares.at(w, t))
                V.tensor_scalar(ssq[:, c], ssq[:, c], 1.0 / D, EPS, ALU.mult, ALU.add).then_inc(*rstd_in.next(w, t))
                dve.wait_ge(*rstd_out.at(w, t))
                link(V.reciprocal(rst[:, c], rst[:, c]))
                if t and not w:
                    dve.wait_ge(*product.at("xT", w, t - 1, 1))
                V.tensor_scalar(xo[:, 0, :], xs[:, t, :], rst[:, c], None, ALU.mult).then_inc(*xn_ready.next(w, t))

            def mod_turn(m):
                job = ("modT", m)
                if m == 0:
                    dve.wait_ge(params_in, 16)
                dve.wait_ge(*product.at(*job))
                V.tensor_tensor(modT[:, 4 * m:4 * m + 4, :], ps(*job)[:, 0:8].rearrange("p (i v) -> p i v", v=2),
                                col(Q[:, Q_BMOD + 4 * m:Q_BMOD + 4 * m + 4], 2), ALU.add
                                ).then_inc(*reads(mod_ready, (m,), *job))

            def scales(w):
                dve.wait_ge(*mod_ready.at((3, 9)[w]))
                q = (Q_NA, Q_NF)[w]
                V.scalar_tensor_tensor(out=scl[:, w, :, :], in0=modT[:, 24 * w + 8:24 * w + 16, :], scalar=1.0,
                                       in1=col(Q[:, q:q + 8], 2), op0=ALU.add, op1=ALU.mult
                                       ).then_inc(*scl_ready.next(w))

            def modulate():
                dve.wait_ge(*scl_ready.at(0))
                for t in (1, 2):
                    dve.wait_ge(*hT_ready.at(0, t, 1))
                    ins = V.tensor_tensor(hT[:, t], hT[:, t], col(scl[:, 0, :, 1], P), ALU.mult)
                link(ins)
                for t in (1, 2):
                    V.tensor_tensor(hT[:, t], hT[:, t], col(modT[:, 0:KD, 1], P), ALU.add
                                    ).then_inc(*modulated.next(t))

            def channels(b):
                dve.wait_ge(*pre_ready.at(b))
                if b >= 3:
                    dve.wait_ge(*silu_ready.at(b - 3))
                o = cy[:, b % 3, :]
                for i in range(TAPS):
                    tap = Q[:, Q_CONV + TAPS * b + i:Q_CONV + TAPS * b + i + 1]
                    src = pre[:, b % 3, i:i + 386]
                    if i == 0:
                        link(V.tensor_scalar(o, src, tap, None, ALU.mult))
                    else:
                        ins = V.scalar_tensor_tensor(out=o, in0=src, scalar=tap, in1=o, op0=ALU.mult, op1=ALU.add)
                        if i < TAPS - 1:
                            link(ins)
                        else:
                            ins.then_inc(*conv_ready.next(b))

            def gate_in():
                dve.wait_ge(consts_in, 32)
                dve.wait_ge(*ba_ready.at(2))
                dve.wait_ge(*ctok_ready.at(7))
                V.tensor_scalar(ssk, ssk, EPS, None, ALU.add).then_inc(*knorm_in.next())
                link(V.tensor_tensor(g2[:, :, :], ba[:, :, 8:16], rep(Q[:, Q_DT:Q_DT + 8], NT), ALU.add))
                V.scalar_tensor_tensor(out=g1[:, :, :], in0=g2[:, :, :], scalar=-1.0, in1=g2[:, :, :],
                                       op0=ALU.mult, op1=ALU.min).then_inc(*softplus_in.next())
                dve.wait_ge(*knorm_out.at())
                link(V.reciprocal(rnk, rnk))
                rn = by_tile(rnk)
                link(V.tensor_scalar(rn[:, :, 0:4], rn[:, :, 0:4], P ** -0.5, None, ALU.mult))
                dve.wait_ge(*softplus_out.at())
                link(V.scalar_tensor_tensor(out=g1[:, :, :], in0=g2[:, :, :], scalar=0.0, in1=g1[:, :, :],
                                            op0=ALU.max, op1=ALU.add))
                V.scalar_tensor_tensor(out=gg[:, :, :], in0=g1[:, :, :], scalar=-1.0, in1=rep(nea, NT),
                                       op0=ALU.mult, op1=ALU.mult).then_inc(*g_ready.next())

            def decay():
                rn = by_tile(rnk)
                for t in range(NT):
                    v = dn_tok[:, t, 0:1024].rearrange("p (b n) -> p b n", n=P)
                    V.tensor_tensor(v, v, col(rn[:, t, :], P), ALU.mult).then_inc(*kscaled.next(t))
                dve.wait_ge(*eg_ready.at())
                dve.wait_ge(*beta_ready.at())
                V.tensor_tensor(bg[:, :, :], beta[:, :, :], eg[:, :, :], ALU.mult).then_inc(*bg_ready.next())

            def gate_rows(w, v, h):
                sq_free()
                o = (16, 40)[w] + 4 * h
                if (v, h) == (0, 0):
                    dve.wait_ge(*mod_ready.at((5, 11)[w]))
                V.tensor_copy(heads(sq[:, :]), col(modT[:, o:o + 4, v], P)).then_inc(*gateb.next(w, v, h))
                sq_reader.append(("gate", w, v, h))

            def lam_step():
                L = [Q[:, Q_LAM + 64 * i:Q_LAM + 64 * (i + 1)] for i in range(4)]
                sq_free()
                V.tensor_tensor_reduce(sq[:, 0:64], L[0], L[1], 1.0, 0.0, ALU.mult, ALU.add, lamv[:, 0:1])
                V.tensor_tensor_reduce(sq[:, 64:128], L[2], L[3], 1.0, 0.0, ALU.mult, ALU.add, lamv[:, 1:2]
                                       ).then_inc(*lam_in.next())
                V.tensor_scalar(sub08, Q[:, Q_SUB:Q_SUB + P], 1.0 - LAM_INIT, None, ALU.mult)
                dve.wait_ge(*lam_exp.at())
                link(V.tensor_scalar(lam[:, 0:1], lamv[:, 3:4], lamv[:, 2:3], -LAM_INIT, ALU.subtract, ALU.add))

            def dn_scale(pi):
                for t, d in PAIRS[pi]:
                    if pi == 0:
                        dve.wait_ge(*product.at("cT", 11))
                        dve.wait_ge(*ctok_ready.at(11))
                    elif pi == 1:
                        dve.wait_ge(*product.at("S", *PAIRS[0][d]))
                    else:
                        dve.wait_ge(*product.at("pq", 3, 0))
                    V.tensor_copy(heads(LT[pi][d]), col(gg[:, t, 4 * d:4 * d + 4], P)).then_inc(*bc_ready.next("g", t, d))
                    V.tensor_copy(heads(PM[pi][d]), col(beta[:, t, 4 * d:4 * d + 4], P)).then_inc(*bc_ready.next("b", t, d))

            def dn_decay(pi):
                for t, d in PAIRS[pi]:
                    job = ("gr", t, d)
                    edge = P - 1 if d == 0 else 0
                    c4 = slice(4 * d, 4 * d + 4)
                    dve.wait_ge(*product.at(*job))
                    dve.wait_ge(*egrow_ready.at(t, d))
                    V.tensor_tensor(heads(DT[pi][d]), heads(ps(*job)[:, :]), col(gc[:, t, c4], P), ALU.subtract)
                    if pi:
                        dve.wait_ge(*kds_ready.at(*PAIRS[pi - 1][d]))
                    V.tensor_tensor(kde[:, c4], heads(ps(*job)[:, :])[:, :, edge], gc[:, t, c4], ALU.subtract
                                    ).then_inc(*reads(kde_ready, (t, d), *job))
                    dve.wait_ge(*kde_ready.at(t, d))
                    V.tensor_tensor(heads(DT[pi][d]), heads(DT[pi][d]), rep(nb[d], 4), ALU.min).then_inc(*dd_ready.next(t, d))

            def dn_scores(pi):
                for t, d in PAIRS[pi]:
                    dve.wait_ge(*dt_ready.at(t, d))
                    dve.wait_ge(*product.at("kk", t, d))
                    V.tensor_tensor(LT[pi][d], ps("kk", t, d)[:, :], DT[pi][d], ALU.mult
                                    ).then_inc(*reads(lt_ready, ("k", t, d), "kk", t, d))
                for t, d in PAIRS[pi]:
                    dve.wait_ge(*product.at("br", t, d))
                    dve.wait_ge(*lt_ready.at("k", t, d))
                    V.scalar_tensor_tensor(out=LT[pi][d], in0=ps("br", t, d)[:, :], scalar=-1.0, in1=LT[pi][d],
                                           op0=ALU.mult, op1=ALU.mult).then_inc(*reads(lt_ready, (t, d), "br", t, d))
                for t, d in PAIRS[pi]:
                    dve.wait_ge(*product.at("qk", t, d))
                    V.tensor_tensor(DT[pi][d], ps("qk", t, d)[:, :], DT[pi][d], ALU.mult
                                    ).then_inc(*reads(at_ready, (t, d), "qk", t, d))

            def dn_p(pi, lv):
                if (pi, lv) == (0, 0):
                    dve.wait_ge(kv_in, 48)
                for t, d in PAIRS[pi]:
                    job = ("P", t, d, lv)
                    dve.wait_ge(*product.at(*job))
                    V.tensor_tensor(heads(PM[pi][d]), heads(ps(*job)[:, :]), rep(level_mask(d, lv), 4), ALU.mult
                                    ).then_inc(*reads(p_ready, (t, d, lv), *job))

            def dn_t(pi, lv):
                for t, d in PAIRS[pi]:
                    if lv == 0:
                        dve.wait_ge(*p_ready.at(t, d, 0))
                        V.tensor_tensor(heads(TM[pi][d]), heads(PM[pi][d]), rep(ident, 4), ALU.add
                                        ).then_inc(*t_ready.next("T", t, d, 0))
                    elif lv < LEVELS - 1:
                        job = ("T", t, d, lv)
                        dve.wait_ge(*product.at(*job))
                        V.tensor_tensor(TM[pi][d], ps(*job)[:, :], TM[pi][d], ALU.add
                                        ).then_inc(*reads(t_ready, job, *job))
                    job = ("TT", t, d, lv)
                    dve.wait_ge(*product.at(*job))
                    if lv == 0:
                        V.tensor_tensor(heads(TT[pi][d]), heads(ps(*job)[:, :]), rep(ident, 4), ALU.add
                                        ).then_inc(*reads(t_ready, job, *job))
                    else:
                        V.tensor_tensor(TT[pi][d], ps(*job)[:, :], TT[pi][d], ALU.add
                                        ).then_inc(*reads(t_ready, job, *job))

            def dn_v(pi):
                for t, d in PAIRS[pi]:
                    job = ("vn", t, d)
                    dve.wait_ge(*product.at(*job))
                    V.tensor_copy(TM[pi][d], ps(*job)[:, :]).then_inc(*reads(vn_ready, (t, d), *job))

            def dn_o(pi):
                for t, d in PAIRS[pi]:
                    job = ("o", t, d)
                    dve.wait_ge(*product.at(*job))
                    out = dn_tok[:, t, 0:512]
                    if (t, d) in ((0, 0), (1, 0), (2, 1)):
                        V.tensor_copy(out, ps(*job)[:, :]).then_inc(*reads(osum_ready, (t, d), *job))
                    else:
                        if t == 0:
                            dve.wait_ge(*osum_ready.at(0, 0))
                        V.tensor_tensor(out, ps(*job)[:, :], out, ALU.add).then_inc(*reads(osum_ready, (t, d), *job))

            def dn_s(pi):
                for t, d in PAIRS[pi]:
                    if updates_state(t, d):
                        job = ("S", t, d)
                        dve.wait_ge(*product.at(*job))
                        if t == 0:
                            dve.wait_ge(*dn_pool.at("kd", 0, 1))
                            V.tensor_copy(S[:, d, :], ps(*job)[:, :]).then_inc(*reads(s_ready, (t, d), *job))
                        else:
                            dve.wait_ge(*dn_pool.at("last", t, d))
                            for h in range(4):
                                s = slice(h * P, (h + 1) * P)
                                ins = V.scalar_tensor_tensor(out=S[:, d, s], in0=S[:, d, s],
                                                             scalar=last[:, 4 * d + h:4 * d + h + 1],
                                                             in1=ps(*job)[:, s], op0=ALU.mult, op1=ALU.add)
                            ins.then_inc(*reads(s_ready, (t, d), *job))

            def expo(t, h):
                nk = P if t == 0 else 3 * P
                for m in range(2):
                    c = slice(2 * h + m, 2 * h + m + 1)
                    dve.wait_ge(*product.at("sc", t, 2 * h + m))
                    ins = V.tensor_reduce(mx[:, c], ps("sc", t, 2 * h + m)[:, 0:nk], AX.X, ALU.max)
                link(ins)
                V.tensor_scalar(nmx[:, 2 * h:2 * h + 2], mx[:, 2 * h:2 * h + 2], -DA_DH ** -0.5, None, ALU.mult
                                ).then_inc(*mx_ready.next(t, h))

            def diff(t, h):
                nk = P if t == 0 else 3 * P
                c, c1 = slice(2 * h, 2 * h + 1), slice(2 * h + 1, 2 * h + 2)
                dve.wait_ge(*e_ready.at(t, 2 * h + 1))
                link(V.reciprocal(rz[:, 2 * h:2 * h + 2], zz[:, 2 * h:2 * h + 2]))
                V.tensor_scalar(rz[:, c1], rz[:, c1], lam[:, 0:1], None, ALU.mult)
                link(V.tensor_scalar(E[:, h % 2, 0, 0:nk], E[:, h % 2, 0, 0:nk], rz[:, c], None, ALU.mult))
                V.scalar_tensor_tensor(out=E[:, h % 2, 0, 0:nk], in0=E[:, h % 2, 1, 0:nk], scalar=rz[:, c1],
                                       in1=E[:, h % 2, 0, 0:nk], op0=ALU.mult, op1=ALU.add
                                       ).then_inc(*a_ready.next(t, h))

            def v_copy(t, h):
                dve.wait_ge(*product.at("av", t, h))
                V.tensor_copy(ocat[:, h * P:(h + 1) * P], ps("av", t, h)[:, 0:P]
                              ).then_inc(*reads(av_ready, (t, h), "av", t, h))

            def head_norm(t, g):
                if g == 0:
                    dve.wait_ge(*av_ready.at(t, 3))
                    src = ocat[:, 0:512]
                else:
                    src = dn_tok[:, t, 0:512]
                    dve.wait_ge(*osum_ready.at(t, (1, 1, 0)[t]))
                    dve.wait_ge(*tok_ready.at(3, t))
                s4 = heads(src)
                sq_free()
                link(V.tensor_tensor(sq[:, :], src, src, ALU.mult))
                link(V.tensor_reduce(ob, heads(sq[:, :]), AX.X, ALU.add))
                V.tensor_scalar(ob, ob, 1.0 / P, EPS, ALU.mult, ALU.add).then_inc(*on_in.next(t, g))
                dve.wait_ge(*on_out.at(t, g))
                link(V.reciprocal(obr, obr))
                link(V.tensor_tensor(s4, s4, col(obr, P), ALU.mult))
                if g == 0:
                    V.tensor_tensor(s4, s4, rep(sub08, 4), ALU.mult).then_inc(*ocat_ready.next(t, 0))
                else:
                    link(V.tensor_tensor(s4, s4, rep(Q[:, Q_DNN:Q_DNN + P], 4), ALU.mult))
                    V.tensor_tensor(ocat[:, 512:1024], src, z[:, t, :], ALU.mult).then_inc(*ocat_ready.next(t, 1))

            def resid(t, h):
                v = min(t, 1)
                dve.wait_ge(*product.at("wo", t, h))
                dve.wait_ge(*gate_ready.at(0, v, h))
                s = slice(h * 512, (h + 1) * 512)
                sq_free()
                V.tensor_tensor(sq[:, :], ps("wo", t, h)[:, :], gate[:, v, s], ALU.mult
                                ).then_inc(*reads(x2_ready, ("g", t, h), "wo", t, h))
                dve.wait_ge(*x2_ready.at("g", t, h))
                V.tensor_tensor(xs[:, t, s], xs[:, t, s], sq[:, :], ALU.add).then_inc(*x2_ready.next(t, h))
                dve.wait_ge(*x2_ready.at(t, h))

            def two_rounds(src, vals, inds):
                for r in range(2):
                    o = slice(8 * r, 8 * r + 8)
                    for s, v in zip(src, vals):
                        ins = V.max(v[:, o], s)
                    link(ins)
                    for s, v, i in zip(src, vals, inds):
                        ins = V.max_index(i[:, o], v[:, o], s)
                    link(ins)
                    if r == 0:
                        for s, v in zip(src, vals):
                            ins = V.match_replace(s, v[:, o], s, NEG)
                        link(ins)

            def blocks(ap, n, first, count):
                return [ap[:, n * b:n * (b + 1)] for b in range(first, first + count)]

            def top_key(i, t):
                dve.wait_ge(*sco_ready.at(i, t))
                two_rounds(blocks(sco(t, i // 2), NKEY, 4 * (i % 2), 4), blocks(sv[t], TOPK, 4 * i, 4),
                           blocks(siu[t], TOPK, 4 * i, 4))

            def pair_sums(t, hh):
                v4 = sv[t][:, 128 * hh:128 * hh + 128].rearrange("p (h i r) -> p h i r", h=H, i=2)
                link(V.tensor_tensor(sco(t, hh).rearrange("p (h a b) -> p h a b", h=H, a=TOPK),
                                     v4[:, :, 0, :].unsqueeze(3).to_broadcast([P, H, TOPK, TOPK]),
                                     v4[:, :, 1, :].unsqueeze(2).to_broadcast([P, H, TOPK, TOPK]), ALU.add))

            def top_pair(t, hh, w):
                two_rounds(blocks(sco(t, hh), TOPK * TOPK, 2 * w, 2), blocks(sv2[t], TOPK, H * hh + 2 * w, 2),
                           blocks(pos[t], TOPK, H * hh + 2 * w, 2))

            def places(t, hh):
                s = slice(64 * hh, 64 * hh + 64)
                s1 = slice(128 + 64 * hh, 128 + 64 * hh + 64)
                v2 = sv2[t][:, s].rearrange("p (h r) -> p h r", h=H)
                if hh == 0 and t:
                    dve.wait_ge(*gx_out.at(t - 1, 1))
                V.tensor_tensor(gex[t][:, s].rearrange("p (h r) -> p h r", h=H), v2,
                                v2[:, :, 0:1].to_broadcast([P, H, TOPK]), ALU.subtract).then_inc(*gx_in.next(t, hh))
                V.tensor_scalar(phl[t][:, s], pos[t][:, s], 4, None, ALU.logical_shift_right)
                link(V.tensor_scalar(phl[t][:, s1], pos[t][:, s], 15, None, ALU.bitwise_and))
                V.tensor_copy(phf[t][:, s], phl[t][:, s])
                V.tensor_copy(phf[t][:, s1], phl[t][:, s1])
                link(V.tensor_copy(sif[t][:, 128 * hh:128 * hh + 128], siu[t][:, 128 * hh:128 * hh + 128]))

            def chosen(t, hh, w):
                i4 = sif[t][:, 128 * hh:128 * hh + 128].rearrange("p (h i r) -> p h i r", h=H, i=2)
                c4 = sco(t, hh).rearrange("p (h a b) -> p h a b", h=H, a=TOPK)
                first = 64 * hh + 128 * w
                ph = phf[t][:, first:first + 64].rearrange("p (h r) -> p h r", h=H)
                link(V.tensor_tensor(c4, ph.unsqueeze(3).to_broadcast([P, H, TOPK, TOPK]),
                                     iota.unsqueeze(1).unsqueeze(1).to_broadcast([P, H, TOPK, TOPK]), ALU.is_equal))
                link(V.tensor_tensor(c4, c4, i4[:, :, w, :].unsqueeze(2).to_broadcast([P, H, TOPK, TOPK]), ALU.mult))
                o = e01[t][:, 128 * hh + 64 * w:128 * hh + 64 * w + 64]
                link(V.tensor_reduce(o.rearrange("p (h r) -> p h r", h=H), c4, AX.X, ALU.add))

            def experts(t, hh):
                a, b = e01[t][:, 128 * hh:128 * hh + 64], e01[t][:, 128 * hh + 64:128 * hh + 128]
                link(V.scalar_tensor_tensor(out=a, in0=a, scalar=float(NKEY), in1=b, op0=ALU.mult, op1=ALU.add))
                link(V.tensor_copy(idx[t][:, 64 * hh:64 * hh + 64], a))

            def slot_gates(t, hh):
                c = slice(64 * hh, 64 * hh + 64)
                g8 = gex[t][:, c].rearrange("p (h r) -> p h r", h=H)
                total, inverse = gsm[t][:, H * hh:H * hh + H], gsm[t][:, 8 + H * hh:8 + H * hh + H]
                dve.wait_ge(*gx_out.at(t, hh))
                link(V.tensor_reduce(total, g8, AX.X, ALU.add))
                link(V.reciprocal(inverse, total))
                V.tensor_tensor(gates[t][:, c].rearrange("p (h r) -> p h r", h=H), g8, col(inverse, TOPK), ALU.mult
                                ).then_inc(*idx_ready.next(t, hh))

            def dot_products(t, r, times):
                dve.wait_ge(rows_in[r], times * (16 * GU))
                for u in range(GU):
                    u_rows = rows[:, r * GU + u, 0:D]
                    ins = V.tensor_tensor_reduce(u_rows, u_rows, h2[:, t, :], 1.0, 0.0, ALU.mult, ALU.add,
                                                 dots[:, r, u:u + 1])
                ins.then_inc(dot_ready, 1)

            def diagonals(t, n, g, r):
                dve.wait_ge(gelu_ready, g + 1)
                for u in range(GU):
                    ins = V.tensor_scalar(diag[:, r * GU + u, :], ident, gel[:, r, u:u + 1],
                                          gates[t][:, bass.ds(n * GU + u, 1)], ALU.mult, ALU.mult)
                ins.then_inc(diag_ready, 1)

            def peer(t, n):
                if (t, n) == (0, 0):
                    dve.wait_ge(*h2_ready.at(0, 1))
                if (t, n) == (1, 0):
                    dve.wait_ge(*h2_ready.at(2, 1))
                g = t * SLOTS + n
                dot_products(t, g % GR, g // GR + 1)
                if n:
                    diagonals(t, n - 1, g - 1, (g - 1) % GR)

            def peer_end(t):
                g = t * SLOTS + SLOTS - 1
                diagonals(t, SLOTS - 1, g, g % GR)

            def last_norm(t):
                v = min(t, 1)
                dve.wait_ge(vsum_done, (t + 1) * SLOTS)
                if t == 0:
                    dve.wait_ge(nout_in, 16)
                    dve.wait_ge(*gate_ready.at(1, 1, 1))
                    sq_free()
                for h in range(2):
                    s = slice(h * 512, (h + 1) * 512)
                    ins = V.tensor_tensor(sq[:, :], acc[h][:, :], gate[:, v, s], ALU.mult)
                    if h:
                        ins.then_inc(*acc_read.next(t))
                        dve.wait_ge(*acc_read.at(t))
                    else:
                        link(ins)
                    link(V.tensor_tensor(xs[:, t, s], xs[:, t, s], sq[:, :], ALU.add))
                link(V.tensor_tensor_reduce(xo[:, 0, :], xs[:, t, :], xs[:, t, :], 1.0, 0.0, ALU.mult, ALU.add, fss))
                V.tensor_scalar(fss, fss, 1.0 / D, EPS, ALU.mult, ALU.add).then_inc(*fin_in.next(t))
                dve.wait_ge(*fin_out.at(t))
                link(V.reciprocal(fr, fr))
                V.scalar_tensor_tensor(out=xs[:, t, :], in0=xs[:, t, :], scalar=fr, in1=xo[:, 1, :],
                                       op0=ALU.mult, op1=ALU.mult).then_inc(*y_ready.next(t))

            run({"norm": norm, "mod_turn": mod_turn, "modulate": modulate, "scales": scales, "channels": channels, "gate_in": gate_in,
                 "decay": decay, "gate": gate_rows, "lam": lam_step, "dn_scale": dn_scale, "dn_decay": dn_decay,
                 "dn_scores": dn_scores, "dn_p": dn_p, "dn_t": dn_t, "dn_v": dn_v, "dn_o": dn_o, "dn_s": dn_s,
                 "expo": expo, "diff": diff, "v_copy": v_copy, "head_norm": head_norm, "resid": resid,
                 "top_key": top_key, "top_pair": top_pair, "pair_sums": pair_sums,
                 "places": places, "chosen": chosen, "experts": experts, "slot_gates": slot_gates,
                 "peer": peer, "peer_end": peer_end, "last_norm": last_norm})
            for t, first in ((1, MIXED), (2, 1)):
                if t == 2:
                    peer(2, 0)
                g0 = t * SLOTS + first
                rounds, rest = in_rounds(first, SLOTS)
                with dve.Fori(0, rounds) as i:
                    for r in range(GR):
                        dot_products(t, (g0 + r) % GR, i + ((g0 + r) // GR + 1))
                        diagonals(t, i * GR + (first + r - 1), i * GR + (g0 + r - 1), (g0 + r - 1) % GR)
                for n in rest:
                    peer(t, n)
                peer_end(t)
                last_norm(t)


_NAMES = ["x", "cst", "msk", "par", "wch", "wba", "kcT", "vc", "s0", "subk", "uv", "nout"]
_OUTS = [("y", (NT, P, D)), ("o_ck", (P, 512)), ("o_cv", (P, 512)), ("o_sf", (P, 512)), ("o_sb", (P, 512))]


def shape_constants():
    k = np.zeros((P, C_END), np.float32)
    i = np.arange(P)
    k[:, C_ID:C_ID + P] = np.eye(P)
    k[:, C_UP:C_UP + P] = i[:, None] <= i[None, :]
    k[:, C_LO:C_LO + P] = i[:, None] >= i[None, :]
    k[:, C_NBF:C_NBF + P] = np.where(i[None, :] >= i[:, None], 0.0, -BIG)
    k[:, C_NBB:C_NBB + P] = np.where(i[None, :] <= i[:, None], 0.0, -BIG)
    n = np.arange(2 * P)
    at = np.stack([n // GRID_W, n % GRID_W], -1).astype(np.float32)
    f = np.power(np.float32(10000.0), -np.arange(0, 32, 2, dtype=np.float32) / np.float32(32)).astype(np.float32)
    ang = (at[:, :, None] * f).astype(np.float32)
    for c, fn in ((C_COS, np.cos), (C_SIN, np.sin)):
        k[:, c:c + 64] = fn(ang).astype(np.float32).reshape(2, P, 32).transpose(1, 0, 2).reshape(P, 64)
    k[:, C_IOTA:C_IOTA + 16] = np.arange(16)
    return k


def level_masks():
    i = np.arange(P)
    out = []
    for lv in range(LEVELS):
        s = 1 << lv
        out.append((i[:, None] // (2 * s) == i[None, :] // (2 * s)) & (i[:, None] // s % 2 == 1)
                   & (i[None, :] // s % 2 == 0))
    return np.concatenate(out + [m.T for m in out], 1).astype(np.uint16) * np.uint16(BF16_ONE)


def _layout(a):
    def cols(v):
        return v.reshape(-1, P).T

    def rows(v):
        return np.broadcast_to(v.reshape(1, -1), (P, v.size))

    f = np.float32
    par = np.empty((P, Q_END), f)
    par[:, Q_C:Q_C + 16] = np.stack([cols(a["c_ctx"]), cols(a["c"][0])], -1).reshape(P, 16)
    par[:, Q_BMOD:Q_BMOD + 48] = cols(a["b_mod"][0])
    par[:, Q_NA:Q_NA + 8] = cols(a["norm_attn"][0])
    par[:, Q_NF:Q_NF + 8] = cols(a["norm_ffn"][0])
    par[:, Q_CONV:Q_CONV + 60] = a["conv_w"][0].reshape(TAPS, 12, P).transpose(2, 1, 0).reshape(P, 60)
    par[:, Q_DNN:Q_DNN + P] = rows(a["dn_norm"])
    par[:, Q_SUB:Q_SUB + P] = rows(a["subln"])
    par[:, Q_ALOG:Q_ALOG + 8] = rows(a["a_log"])
    par[:, Q_DT:Q_DT + 8] = rows(a["dt_bias"])
    for i, n in enumerate(("lambda_q1", "lambda_k1", "lambda_q2", "lambda_k2")):
        par[:, Q_LAM + 64 * i:Q_LAM + 64 * i + 64] = rows(a[n])
    w_in = a["w_in"][0]
    mats = {"mod": a["w_mod"][0], "da": w_in[:, 0:1536], "dn": w_in[:, 1536:3072], "z": w_in[:, 3072:3584],
            "out": a["w_out"][0], "pq": a["w_pq"][0]}
    wch = np.empty((len(STORED), P, KD, CH), f)
    for n, (kind, i, _) in enumerate(STORED):
        wch[n] = mats[kind][:, i * CH:(i + 1) * CH].reshape(KD, P, CH).transpose(1, 0, 2)
    uv = np.empty((a["expert_u"].shape[1], 2 * D), f)
    uv[:, :D] = a["expert_u"][0]
    uv[:, D:] = a["expert_v"][0]
    x = np.concatenate([a["x_prompt"][0], a["x_sample"][0]], 0).reshape(NT, P, D).transpose(1, 0, 2)
    s0 = np.stack([a["state_fwd"][0, 0], a["state_bwd"][0, 0]], 0)
    return {
        "x": x, "cst": shape_constants(), "msk": level_masks(), "par": par, "wch": wch,
        "wba": w_in[:, 3584:3600].reshape(KD, P, 16).transpose(1, 0, 2),
        "kcT": a["cache_k"][0, 0].reshape(P, DA_H, P).transpose(2, 1, 0),
        "vc": a["cache_v"][0, 0].reshape(P, 512),
        "s0": s0.transpose(2, 0, 1, 3).reshape(P, 2, 512),
        "subk": a["sub_keys"][0].reshape(4, 4, NKEY, P).transpose(0, 3, 1, 2).reshape(4, P, 512),
        "uv": uv, "nout": rows(a["norm_out"]),
    }


def kernel(**inputs):
    import concourse.bacc as _bacc
    from concourse.bass_utils import run_bass_kernel_spmd as _run

    a = {k: np.asarray(v) for k, v in inputs.items()}
    data = {k: np.ascontiguousarray(v) for k, v in _layout(a).items()}
    counts = Counts()
    for _ in range(2):
        nc = _bacc.Bacc("TRN2", target_bir_lowering=False, num_devices=1)
        args = [nc.dram_tensor(f"in_{n}", data[n].shape, mybir.dt.from_np(data[n].dtype), kind="ExternalInput").ap() for n in _NAMES]
        args += [nc.dram_tensor(f"out_{n}", s, mybir.dt.float32, kind="ExternalOutput").ap() for n, s in _OUTS]
        program(nc, counts, *args)
    r = _run(nc, [{f"in_{n}": data[n] for n in _NAMES}], core_ids=[0])
    got = {n: r.results[0][f"out_{n}"] for n, _ in _OUTS}
    y = got["y"].reshape(T, D)

    def state(s):
        return s.reshape(P, DN_H, P).transpose(1, 0, 2).reshape(1, 1, DN_H, P, P)

    return (y[:P].reshape(1, P, D), y[P:].reshape(1, 2 * P, D), got["o_ck"].reshape(1, 1, P, 2 * DA_H, DA_DH),
            got["o_cv"].reshape(1, 1, P, DA_H, 2 * DA_DH), state(got["o_sf"]), state(got["o_sb"]))
```
